# Optimizing a Trainium2 kernel written in Bass

```python
import math
import jax, jax.numpy as jnp
from jax import lax
import numpy as np

D_MODEL = 1024
BATCH = 1
SEQ = 256
DEPTH = 2

N_HEADS = 8
HEAD_DIM = D_MODEL // N_HEADS
ROT_DIM = HEAD_DIM // 4
ROPE_THETA = 500000.0
D_FF = ((8 * D_MODEL // 3 + 255) // 256) * 256
MOBA_BLOCK = 256
MOBA_TOPK = 3
MOBA_Q_CHUNK = 64
SB_Q_BLOCK = 128
N_A_LAYERS = DEPTH // 2
N_B_LAYERS = DEPTH - N_A_LAYERS
DEEPNORM_ALPHA = (2.0 * DEPTH) ** 0.25
DEEPNORM_BETA = (8.0 * DEPTH) ** -0.25
LN_EPS = 1e-5
N_SUB = 3
NEG_INF = -1e30

kernel_name = 'yoco_moba_stickbreak_macaron_deepnorm_adaln'

def layer_norm(x, g, b):
    xf = x.astype(jnp.float32)
    mu = jnp.mean(xf, axis=-1, keepdims=True)
    var = jnp.mean(jnp.square(xf - mu), axis=-1, keepdims=True)
    return ((xf - mu) * lax.rsqrt(var + LN_EPS) * g.astype(jnp.float32) + b.astype(jnp.float32)).astype(x.dtype)

def modulate(x, shift, scale):
    return x * (1.0 + scale[:, None, :]) + shift[:, None, :]

def post_norm_residual(x, y, gate, weight, g, b):
    return layer_norm(DEEPNORM_ALPHA * x + weight * (1.0 + gate[:, None, :]) * y, g, b)

def swiglu(h, w_in, w_out):
    g, u = jnp.split(h @ w_in, 2, axis=-1)
    return (jax.nn.silu(g) * u) @ w_out

def split_heads(t):
    b, s, _ = t.shape
    return t.reshape(b, s, N_HEADS, HEAD_DIM).transpose(0, 2, 1, 3)

def merge_heads(t):
    b, h, s, d = t.shape
    return t.transpose(0, 2, 1, 3).reshape(b, s, h * d)

def partial_rotary(t, pos):
    half = ROT_DIM // 2
    inv_freq = jnp.power(ROPE_THETA, -jnp.arange(half, dtype=jnp.float32) * 2.0 / ROT_DIM)
    ang = pos.astype(jnp.float32)[:, None] * inv_freq[None, :]
    cos = jnp.cos(ang)[None, None]
    sin = jnp.sin(ang)[None, None]
    tr = t[..., :ROT_DIM].astype(jnp.float32)
    t1, t2 = tr[..., :half], tr[..., half:]
    rot = jnp.concatenate([t1 * cos - t2 * sin, t2 * cos + t1 * sin], axis=-1).astype(t.dtype)
    return jnp.concatenate([rot, t[..., ROT_DIM:]], axis=-1)

def _moba_one_sequence(q_b, kb_b, vb_b, idx_b, k_own_b, v_own_b, own_mask, scale):
    h, qc, n_sel = idx_b.shape
    heads = jnp.arange(h)[:, None, None]
    kg = kb_b[heads, idx_b]
    vg = vb_b[heads, idx_b]
    s_sel = jnp.einsum('hqd,hqjkd->hqjk', q_b, kg).reshape(h, qc, -1).astype(jnp.float32) * scale
    s_own = jnp.einsum('hqd,hkd->hqk', q_b, k_own_b).astype(jnp.float32) * scale
    s_own = jnp.where(own_mask[None], s_own, NEG_INF)
    p = jax.nn.softmax(jnp.concatenate([s_sel, s_own], axis=-1), axis=-1).astype(vg.dtype)
    n_k = n_sel * MOBA_BLOCK
    p_sel = p[..., :n_k].reshape(h, qc, n_sel, MOBA_BLOCK)
    p_own = p[..., n_k:]
    return (jnp.einsum('hqjk,hqjkd->hqd', p_sel, vg)
            + jnp.einsum('hqk,hkd->hqd', p_own, v_own_b))

def moba_attention(q, k, v):
    b, h, s, dh = q.shape
    scale = dh ** -0.5
    n_full = s // MOBA_BLOCK
    kbar = k[:, :, :n_full * MOBA_BLOCK].reshape(b, h, n_full, MOBA_BLOCK, dh).astype(jnp.float32).mean(axis=3)
    outs = []
    for t0 in range(0, s, MOBA_Q_CHUNK):
        cur = t0 // MOBA_BLOCK
        own_lo = cur * MOBA_BLOCK
        own_hi = min(own_lo + MOBA_BLOCK, s)
        q_c = q[:, :, t0:t0 + MOBA_Q_CHUNK]
        k_own = k[:, :, own_lo:own_hi]
        v_own = v[:, :, own_lo:own_hi]
        own_mask = (own_lo + jnp.arange(own_hi - own_lo))[None, :] <= (t0 + jnp.arange(MOBA_Q_CHUNK))[:, None]
        n_sel = min(MOBA_TOPK, cur)
        if n_sel == 0:
            sc = jnp.einsum('bhqd,bhkd->bhqk', q_c, k_own).astype(jnp.float32) * scale
            p = jax.nn.softmax(jnp.where(own_mask[None, None], sc, NEG_INF), axis=-1).astype(v.dtype)
            outs.append(jnp.einsum('bhqk,bhkd->bhqd', p, v_own))
        else:
            gate = jnp.einsum('bhqd,bhnd->bhqn', q_c.astype(jnp.float32), kbar[:, :, :cur])
            _, idx = lax.top_k(gate, n_sel)
            kb = k[:, :, :cur * MOBA_BLOCK].reshape(b, h, cur, MOBA_BLOCK, dh)
            vb = v[:, :, :cur * MOBA_BLOCK].reshape(b, h, cur, MOBA_BLOCK, dh)
            o = lax.map(lambda a: _moba_one_sequence(a[0], a[1], a[2], a[3], a[4], a[5], own_mask, scale),
                        (q_c, kb, vb, idx, k_own, v_own))
            outs.append(o)
    return jnp.concatenate(outs, axis=2)

def stick_breaking_attention(q, k, v):
    b, h, s, dh = q.shape
    scale = dh ** -0.5
    outs = []
    for t0 in range(0, s, SB_Q_BLOCK):
        t1 = t0 + SB_Q_BLOCK
        z = jnp.einsum('bhqd,bhkd->bhqk', q[:, :, t0:t1], k[:, :, :t1]).astype(jnp.float32) * scale
        strict = jnp.arange(t1)[None, :] < (t0 + jnp.arange(SB_Q_BLOCK))[:, None]
        log_keep = jnp.where(strict, jax.nn.log_sigmoid(-z), 0.0)
        log_after = lax.cumsum(log_keep, axis=3, reverse=True) - log_keep
        w = jnp.where(strict, jnp.exp(jax.nn.log_sigmoid(z) + log_after), 0.0)
        outs.append(jnp.einsum('bhqk,bhkd->bhqd', w.astype(v.dtype), v[:, :, :t1]))
    return jnp.concatenate(outs, axis=2)

def setup_inputs(seed: int = 0) -> dict:
    key = jax.random.key(seed)
    ks = jax.random.split(key, 14)
    d, f = D_MODEL, D_FF
    nrm = jax.random.normal
    return {
        'x': nrm(ks[0], (BATCH, SEQ, d), jnp.float32),
        'c': nrm(ks[1], (BATCH, d), jnp.float32),
        'w_ada': nrm(ks[2], (DEPTH, d, 3 * N_SUB * d), jnp.float32) * (0.1 * d ** -0.5),
        'b_ada': nrm(ks[3], (DEPTH, 3 * N_SUB * d), jnp.float32) * 0.01,
        'ln_g': 1.0 + 0.02 * nrm(ks[4], (DEPTH, N_SUB, d), jnp.float32),
        'ln_b': 0.02 * nrm(ks[5], (DEPTH, N_SUB, d), jnp.float32),
        'w_ffn_in': nrm(ks[6], (DEPTH, 2, d, 2 * f), jnp.float32) * d ** -0.5,
        'w_ffn_out': nrm(ks[7], (DEPTH, 2, f, d), jnp.float32) * (f ** -0.5 * DEEPNORM_BETA),
        'w_qkv_a': nrm(ks[8], (N_A_LAYERS, d, 3 * d), jnp.float32) * d ** -0.5,
        'w_q_b': nrm(ks[9], (N_B_LAYERS, d, d), jnp.float32) * d ** -0.5,
        'w_kv_ada': nrm(ks[10], (d, 2 * d), jnp.float32) * (0.1 * d ** -0.5),
        'b_kv_ada': nrm(ks[11], (2 * d,), jnp.float32) * 0.01,
        'w_kv_b': nrm(ks[12], (d, 2 * d), jnp.float32) * d ** -0.5,
        'w_o': nrm(ks[13], (DEPTH, d, d), jnp.float32) * (d ** -0.5 * DEEPNORM_BETA),
    }

def reference(x, c, w_ada, b_ada, ln_g, ln_b, w_ffn_in, w_ffn_out, w_qkv_a, w_q_b,
              w_kv_ada, b_kv_ada, w_kv_b, w_o):
    b, s, d = x.shape
    pos = jnp.arange(s)
    cond = jax.nn.silu(c)
    k_sh = None
    v_sh = None
    for l in range(DEPTH):
        if l == N_A_LAYERS:
            kv_mod = (cond @ w_kv_ada + b_kv_ada).reshape(b, 2, d)
            kv = modulate(x, kv_mod[:, 0], kv_mod[:, 1]) @ w_kv_b
            k_sh, v_sh = jnp.split(kv, 2, axis=-1)
            k_sh = split_heads(k_sh)
            v_sh = split_heads(v_sh)
        mod = (cond @ w_ada[l] + b_ada[l]).reshape(b, 3 * N_SUB, d)
        h = modulate(x, mod[:, 0], mod[:, 1])
        x = post_norm_residual(x, swiglu(h, w_ffn_in[l, 0], w_ffn_out[l, 0]), mod[:, 2], 0.5, ln_g[l, 0], ln_b[l, 0])
        h = modulate(x, mod[:, 3], mod[:, 4])
        if l < N_A_LAYERS:
            q, k, v = jnp.split(h @ w_qkv_a[l], 3, axis=-1)
            q = partial_rotary(split_heads(q), pos)
            k = partial_rotary(split_heads(k), pos)
            y = moba_attention(q, k, split_heads(v))
        else:
            q = split_heads(h @ w_q_b[l - N_A_LAYERS])
            y = stick_breaking_attention(q, k_sh, v_sh)
        y = merge_heads(y) @ w_o[l]
        x = post_norm_residual(x, y, mod[:, 5], 1.0, ln_g[l, 1], ln_b[l, 1])
        h = modulate(x, mod[:, 6], mod[:, 7])
        x = post_norm_residual(x, swiglu(h, w_ffn_in[l, 1], w_ffn_out[l, 1]), mod[:, 8], 0.5, ln_g[l, 2], ln_b[l, 2])
    return x


_drawn_inputs = setup_inputs


def setup_inputs(seed=0):
    import zlib

    import numpy as np

    out = dict(_drawn_inputs(seed))
    spreads = {}
    factors = {'b_ada': 8.0, 'b_kv_ada': 8.0}
    for name, (base, spread) in spreads.items():
        noise = np.random.default_rng([zlib.crc32(name.encode()), seed]).standard_normal(out[name].shape)
        drawn = base * np.exp(spread * noise) if base else spread * noise
        out[name] = __import__('jax').numpy.asarray(drawn.astype(out[name].dtype))
    for name, factor in factors.items():
        out[name] = (out[name] * factor).astype(out[name].dtype)
    return out
```

```python
import math
from contextlib import ExitStack

import numpy as np

import concourse.bass as bass
from concourse import mybir

F32 = mybir.dt.float32
F32R = mybir.dt.float32r
ACT = mybir.ActivationFunctionType
ALU = mybir.AluOpType
AX = mybir.AxisListType

P = 128
D = 1024
SEQ = 256
KT = D // P
TT = SEQ // P
HEADS = 8
DH = D // HEADS
ROT = DH // 4
DFF = 2816
STEPS = DFF // 256
DEPTH = 2
ALPHA = (2.0 * DEPTH) ** 0.25
EPS = 1e-5
SCALE = DH ** -0.5
CH = 2048
RAW = 6
SPL = 3
MODS = 9

FFN_CHUNKS = 3 * STEPS
N_FFN = [0] * 4
N_FFN[0] = 0
N_QKV = N_FFN[0] + FFN_CHUNKS
N_WO = [N_QKV + 12, 0]
N_FFN[1] = N_WO[0] + 4
N_KV = N_FFN[1] + FFN_CHUNKS
N_FFN[2] = N_KV + 8
N_Q = N_FFN[2] + FFN_CHUNKS
N_WO[1] = N_Q + 4
N_FFN[3] = N_WO[1] + 4
N_ALL = N_FFN[3] + FFN_CHUNKS

U_KV = MODS
U_L = [0, MODS + 2]
UNITS = 2 * MODS + 2


def unit(layer, j):
    return U_L[layer] + j


H_OF = [(unit(0, 0), unit(0, 1), None),
        (unit(0, 3), unit(0, 4), 0),
        (unit(0, 6), unit(0, 7), 1),
        (U_KV, U_KV + 1, 2),
        (unit(1, 0), unit(1, 1), None),
        (unit(1, 3), unit(1, 4), 3),
        (unit(1, 6), unit(1, 7), 4)]
GATE_OF = [unit(0, 2), unit(0, 5), unit(0, 8), unit(1, 2), unit(1, 5), unit(1, 8)]
GATE_W = [0.5, 1.0, 0.5, 0.5, 1.0, 0.5]
C_ID, C_TRI, C_CAUSAL, C_STRICT, C_KEEP, C_COS, C_SIN, C_ROT = (
    0, 128, 256, 384, 512, 640, 896, 1152)
C_ALL = 1280
NORM_OF_FFN = [0, 2, 3, 5]
LAST_CHUNK = [N_FFN[0] + FFN_CHUNKS - 1, N_WO[0] + 3, N_FFN[1] + FFN_CHUNKS - 1,
              N_FFN[2] + FFN_CHUNKS - 1, N_WO[1] + 3, N_FFN[3] + FFN_CHUNKS - 1]
H_OF_FFN = [0, 2, 4, 6]


def build(nc, x, c, w_ada, b_ada, ln_g, ln_b, w_ffn_in, w_ffn_out, w_qkv_a, w_q_b,
          w_kv_ada, b_kv_ada, w_kv_b, w_o, consts, out):
    ctx = ExitStack()
    with ctx:
        def sb(name, shape, dt=F32):
            return ctx.enter_context(nc.sbuf_tensor(name, shape, dt))

        def sem(name):
            return ctx.enter_context(nc.semaphore(name))

        raw = sb("raw", [P, RAW, CH])
        w_hi = sb("w_hi", [P, SPL, CH], F32R)
        w_lo = sb("w_lo", [P, SPL, CH], F32R)
        ada = sb("ada", [P, 2, 2, 1024])
        acc = sb("acc", [P, 1024])
        bias0 = sb("bias0", [P, 1024])
        x_sb = sb("x_sb", [P, TT, D])
        hT_hi = sb("hT_hi", [P, KT, SEQ], F32R)
        hT_lo = sb("hT_lo", [P, KT, SEQ], F32R)
        a_hi = sb("a_hi", [P, 2, 2, SEQ], F32R)
        a_lo = sb("a_lo", [P, 2, 2, SEQ], F32R)
        tmp = sb("tmp", [P, 1536])
        h_full = sb("h_full", [P, KT, P])
        gate = sb("gate", [P, D])
        g_row = sb("g_row", [P, D])
        b_row = sb("b_row", [P, D])
        qT = sb("qT", [P, HEADS, SEQ])
        kT = sb("kT", [P, HEADS, SEQ])
        v_sb = sb("v_sb", [P, TT, D])
        cst = sb("cst", [P, C_ALL])
        modT = sb("modT", [P, UNITS, KT])
        coef = sb("coef", [P, len(H_OF), 2, KT])
        lnT = sb("lnT", [P, 2, 48])
        cond = sb("cond", [P, 8])
        stats = sb("stats", [P, TT, 2, 6])
        mv = sb("mv", [P, TT, 2])
        sd = sb("sd", [P, TT])
        rstd = sb("rstd", [P, TT])
        all_ones = sb("all_ones", [P, P])
        neg_ones = sb("neg_ones", [P, P])
        zeros = sb("zeros", [P, 512], mybir.dt.bfloat16)
        eps_t = sb("eps_t", [P, 1])
        mx = sb("mx", [P, HEADS, 2])
        nmx = sb("nmx", [P, HEADS, 2])
        rs = sb("rs", [P, HEADS, 2])
        rinv = sb("rinv", [P, HEADS, 2])

        ident = cst[:, C_ID:C_ID + P]
        tri = cst[:, C_TRI:C_TRI + P]
        causal = cst[:, C_CAUSAL:C_CAUSAL + P]
        strict = cst[:, C_STRICT:C_STRICT + P]
        keep = cst[:, C_KEEP:C_KEEP + P]
        cos_t = cst[0:ROT, C_COS:C_COS + SEQ]
        sin_t = cst[0:ROT, C_SIN:C_SIN + SEQ]
        rot_m = cst[0:ROT, C_ROT:C_ROT + P]
        silu_t = tmp[:, 0:512].rearrange("p (j t) -> p j t", j=2)
        a_full = tmp[:, 512:1024].rearrange("p (j t) -> p j t", j=2)
        prob = tmp[:, 0:768].rearrange("p (j t) -> p j t", j=2)
        sp_t = tmp[:, 768:1536].rearrange("p (j t) -> p j t", j=2)
        rope_t = tmp[0:ROT, 1024:1536]
        z = qT[:, :, :].rearrange("p (t h) s -> p t (h s)", t=TT)
        h_fulls = [h_full[:, :, :], tmp[:, 0:1024].rearrange("p (k t) -> p k t", k=KT)]

        psum = ctx.enter_context(nc.psum_tensor("psum", [P, 8, 512], F32))
        gu = [psum[:, 0, :], psum[:, 1, :]]
        misc = [psum[:, 2, :], psum[:, 3, :]]
        misc2 = psum[:, 2:4, :].rearrange("p b n -> p (b n)")
        y = [psum[:, 4 + i, :] for i in range(4)]
        y_tok = [psum[:, 4 + 2 * t:6 + 2 * t, :].rearrange("p b n -> p (b n)") for t in range(TT)]
        tr_bank = [misc, gu]

        raw_in = [sem(f"raw_in{i}") for i in range(RAW)]
        w_hi_ready = sem("w_hi_ready")
        w_lo_ready = sem("w_lo_ready")
        w_used = sem("w_used")
        ada_in = [sem(f"ada_in{i}") for i in range(2)]
        bias_in = sem("bias_in")
        acc_steps = sem("acc_steps")
        unit_summed = sem("unit_summed")
        mod_ready = sem("mod_ready")
        cst_in = sem("cst_in")
        x_in = sem("x_in")
        c_in = sem("c_in")
        lnT_in = sem("lnT_in")
        set_up = sem("set_up")
        cond_ready = sem("cond_ready")
        lnT_turned = sem("lnT_turned")
        lnT_ready = sem("lnT_ready")
        ln_row_in = sem("ln_row_in")
        turned = sem("turned")
        h_act = sem("h_act")
        h_dve = sem("h_dve")
        h_hi_ready = sem("h_hi_ready")
        h_lo_ready = sem("h_lo_ready")
        coef_ready = sem("coef_ready")
        gu_ready = sem("gu_ready")
        silu_ready = sem("silu_ready")
        a_ready = sem("a_ready")
        a_hi_ready = sem("a_hi_ready")
        a_lo_ready = sem("a_lo_ready")
        diag_ready = sem("diag_ready")
        gate_spread = sem("gate_spread")
        gate_ready = sem("gate_ready")
        y_ready = sem("y_ready")
        dve_step = sem("dve_step")
        var_ready = sem("var_ready")
        sd_ready = sem("sd_ready")
        xn_ready = sem("xn_ready")
        x_ready = sem("x_ready")
        out_done = sem("out_done")
        proj_kept = sem("proj_kept")
        rot_ready = sem("rot_ready")
        rope_done = sem("rope_done")
        score_ready = sem("score_ready")
        nmax_ready = sem("nmax_ready")
        exp_done = sem("exp_done")
        prob_ready = sem("prob_ready")
        probT_ready = sem("probT_ready")
        probT_kept = sem("probT_kept")
        pv_ready = sem("pv_ready")
        yT_hi_ready = sem("yT_hi_ready")
        yT_lo_ready = sem("yT_lo_ready")
        z_ready = sem("z_ready")
        abs_done = sem("abs_done")
        expn_done = sem("expn_done")
        ln1p_done = sem("ln1p_done")
        keepsum_ready = sem("keepsum_ready")
        stick_ready = sem("stick_ready")
        weight_ready = sem("weight_ready")

        block = ctx.enter_context(nc.Block())

        def rows_by_tile(w):
            return w.rearrange("(k p) n -> p k n", p=P)

        def ada_view(w):
            return w.rearrange("(p k) n -> p k n", k=8)

        def columns_chunk(w, start):
            return rows_by_tile(w)[:, :, bass.ds(start, 256)]

        def rows_chunk(w, start):
            return w[bass.ds(start, 256), :].rearrange("(j p) n -> p j n", p=P)

        PROJ = ([(N_QKV + i, w_qkv_a[0], 256 * i) for i in range(12)],
                [(N_KV + i, w_kv_b, 256 * i) for i in range(8)],
                [(N_Q + i, w_q_b[0], 256 * i) for i in range(4)])

        @block.sync
        def _(sp):
            def load(n, src, k, at=None):
                if at is not None or n >= RAW:
                    sp.wait_ge(w_lo_ready, n - RAW + 1 if at is None else at + (n - RAW + 1))
                sp.dma_start(raw[:, n % RAW, :].rearrange("p (k n) -> p k n", k=k), src)\
                  .then_inc(raw_in[n % RAW], 16)

            def load_step(w_in, w_out, n, s, b=None):
                at, c = (None, 0) if b is None else (6 * b, 512 * b)
                load(n + 3 * s - 1, columns_chunk(w_in, c + 256 * s), 8, at)
                load(n + 3 * s, columns_chunk(w_in, c + (DFF + 256 * s)), 8, at)
                load(n + 3 * s + 1, rows_chunk(w_out, c + 256 * (s - 1)), 2, at)

            def load_ffn(f):
                w_in, w_out, n = w_ffn_in[f // 2, f % 2], w_ffn_out[f // 2, f % 2], N_FFN[f]
                load(n, columns_chunk(w_in, 0), 8)
                load(n + 1, columns_chunk(w_in, DFF), 8)
                peeled = 2 if f == 0 else 0
                for s in range(1, 1 + peeled):
                    load_step(w_in, w_out, n, s)
                with sp.Fori(0, (STEPS - 1 - peeled) // 2) as b:
                    for s in (1 + peeled, 2 + peeled):
                        load_step(w_in, w_out, n, s, b)
                load(n + FFN_CHUNKS - 1, rows_chunk(w_out, DFF - 256), 2)

            def load_wo(layer):
                for j in range(4):
                    load(N_WO[layer] + j, rows_chunk(w_o[layer], 256 * j), 2)

            for t in range(TT):
                sp.dma_start(x_sb[:, t, :], x[0, t * P:(t + 1) * P, :]).then_inc(x_in, 16)
            sp.dma_start(cst[:, :], consts).then_inc(cst_in, 16)
            sp.wait_ge(acc_steps, 4)
            load_ffn(0)
            for n, w, at in PROJ[0]:
                load(n, columns_chunk(w, at), 8)
            load_wo(0)
            load_ffn(1)
            for n, w, at in PROJ[1]:
                load(n, columns_chunk(w, at), 8)
            load_ffn(2)
            for n, w, at in PROJ[2]:
                load(n, columns_chunk(w, at), 8)
            load_wo(1)
            load_ffn(3)
            for t in range(TT):
                sp.wait_ge(x_ready, 2 * 5 + t + 1)
                sp.dma_start(out[0, t * P:(t + 1) * P, :], x_sb[:, t, :]).then_inc(out_done, 16)
            sp.wait_ge(out_done, 32)

        @block.gpsimd
        def _(pool):
            def load_unit(w, b, j, u, first=False):
                if not first:
                    pool.wait_ge(acc_steps, 8 * u - 7)
                pool.dma_start(bias0[0:1, :], b[bass.ds(j * 1024, 1024)].rearrange("(a n) -> a n", a=1))\
                    .then_inc(bias_in, 16)
                for q in range(4):
                    if not first or q >= 2:
                        pool.wait_ge(acc_steps, 8 * u + 2 * q - 2)
                    pool.dma_start(ada[:, q % 2, :, :],
                                   ada_view(w)[:, 2 * q:2 * q + 2, bass.ds(j * 1024, 1024)])\
                        .then_inc(ada_in[q % 2], 16)

            pool.wait_ge(set_up, 1)
            load_unit(w_ada[0], b_ada[0], 0, 0, first=True)
            for j in range(1, MODS):
                load_unit(w_ada[0], b_ada[0], j, j)
            for j in range(2):
                load_unit(w_kv_ada, b_kv_ada, j, j + U_KV)
            for j in range(MODS):
                load_unit(w_ada[1], b_ada[1], j, j + U_L[1])

        @block.scalar
        def _(act):
            def split_hi(n, at=0, turn=0):
                act.wait_ge(raw_in[n % RAW], 16 * (n // RAW + 1) + 16 * turn)
                if n >= SPL:
                    act.wait_ge(w_used, n + at - SPL + 1)
                nc.scalar.activation(w_hi[:, n % SPL, :], raw[:, n % RAW, :], ACT.Copy).then_inc(w_hi_ready, 1)

            def ffn_step(f, n, s, splits=3, at=0, turn=0):
                for t in range(2):
                    j = 2 * STEPS * f + 2 * s + t
                    if t == 0:
                        act.wait_ge(gu_ready, STEPS * f + s + 1 + 2 * turn)
                    else:
                        act.wait_ge(w_used, (n + 3 * s if s else n + 1) + 1 + at)
                    nc.scalar.activation(silu_t[:, t, :], gu[t][:, 0:SEQ], ACT.Silu).then_inc(silu_ready, 1)
                    act.wait_ge(a_ready, j + 1 + 4 * turn)
                    nc.scalar.activation(a_hi[:, s % 2, t, :], a_full[:, t, :], ACT.Copy).then_inc(a_hi_ready, 1)
                    if t < splits:
                        split_hi(n + 3 * s + 2 + t, at, turn)
                if splits == 3:
                    split_hi(n + 3 * s + 4, at, turn)

            def ffn(f):
                n = N_FFN[f]
                ffn_step(f, n, 0)
                load_ln_rows(NORM_OF_FFN[f])
                last = f == 3
                with act.Fori(0, STEPS // 2 - (1 if last else 0)) as b:
                    for j in range(2):
                        ffn_step(f, n, 1 + j, at=6 * b, turn=b)
                if last:
                    ffn_step(f, n, STEPS - 2)
                    ffn_step(f, n, STEPS - 1, splits=1)
                nc.scalar.preload_act_table(ACT.Sqrt)
                keep_gate(NORM_OF_FFN[f])

            def load_ln_rows(i):
                if i:
                    act.wait_ge(x_ready, 2 * i)
                act.dma_start(g_row[:, :], ln_g[i // 3, i % 3, :].partition_broadcast(P)).then_inc(ln_row_in, 16)
                act.dma_start(b_row[:, :], ln_b[i // 3, i % 3, :].partition_broadcast(P)).then_inc(ln_row_in, 16)

            def keep_gate(i):
                act.wait_ge(gate_spread, i + 1)
                nc.scalar.activation(gate[:, :], misc2, ACT.Copy, scale=GATE_W[i], bias=GATE_W[i])\
                  .then_inc(gate_ready, 1)

            def h_tile(i, t):
                act.wait_ge(turned, 4 * i + 2 * t + 1)
                act.wait_ge(coef_ready, i + 1)
                for k in range(KT // 2):
                    last = nc.scalar.activation(h_fulls[t][:, k, :], tr_bank[t][0][:, k * P:(k + 1) * P], ACT.Identity,
                                                scale=coef[:, i, 0, k:k + 1], bias=coef[:, i, 1, k:k + 1])
                last.then_inc(h_act, 1)
                act.wait_ge(h_act, 2 * i + t + 1)
                nc.scalar.activation(hT_hi[:, 0:4, t * P:(t + 1) * P], h_fulls[t][:, 0:4, :], ACT.Copy)\
                  .then_inc(h_hi_ready, 1)
                act.wait_ge(h_dve, 2 * i + t + 1)
                nc.scalar.activation(hT_hi[:, 4:8, t * P:(t + 1) * P], h_fulls[t][:, 4:8, :], ACT.Copy)\
                  .then_inc(h_hi_ready, 1)

            def norm(i, h):
                for t in range(TT):
                    act.wait_ge(var_ready, 2 * i + t + 1)
                    nc.scalar.activation(sd[:, t:t + 1], mv[:, t, 1:2], ACT.Sqrt, bias=eps_t[:, 0:1])\
                      .then_inc(sd_ready, 1)
                    if h is not None:
                        h_tile(h, t)

            def keep_yT(layer, h):
                act.wait_ge(pv_ready, HEADS * layer + h + 1)
                nc.scalar.activation(hT_hi[:, h, :], gu[h % 2][:, 0:SEQ], ACT.Copy).then_inc(yT_hi_ready, 1)

            act.dma_start(cond[:, :], c.rearrange("a (p k) -> p (a k)", k=8)).then_inc(c_in, 16)
            for r, w in enumerate((ln_g, ln_b)):
                act.dma_start(tmp[0:48, r * P:(r + 1) * P], w.rearrange("l s (k p) -> (l s k) p", p=P))\
                   .then_inc(lnT_in, 16)
            act.wait_ge(c_in, 16)
            nc.scalar.activation(cond[:, :], cond[:, :], ACT.Silu).then_inc(cond_ready, 1)
            act.wait_ge(lnT_turned, 1)
            nc.scalar.activation(lnT[:, :, :], misc[1][:, 0:96].rearrange("p (r n) -> p r n", r=2), ACT.Copy)\
              .then_inc(lnT_ready, 1)
            split_hi(0)
            split_hi(1)
            h_tile(0, 0)
            h_tile(0, 1)
            ffn(0)
            norm(0, 1)
            n = N_QKV
            for i in range(8):
                split_hi(n + i + 2)
                if i == 1:
                    load_ln_rows(1)
                act.wait_ge(w_used, n + i + 1)
                if i == 0:
                    act.wait_ge(x_ready, 2)
                nc.scalar.activation((qT, kT)[i // 4][:, 2 * (i % 4):2 * (i % 4) + 2, :],
                                     gu[i % 2].rearrange("p (h t) -> p h t", h=2), ACT.Copy).then_inc(proj_kept, 1)
            nc.scalar.preload_act_table(ACT.Exp)

            def soft_exp(h):
                act.wait_ge(nmax_ready, h + 1)
                if h >= 2:
                    act.wait_ge(probT_ready, h - 1)
                nc.scalar.activation(prob[:, h % 2, 0:P], y[h % 2][:, 0:P], ACT.Exp, scale=SCALE,
                                     bias=nmx[:, h, 0:1], accum_out=rs[:, h, 0:1])
                nc.scalar.activation(prob[:, h % 2, P:384], y[h % 2][:, P:384], ACT.Exp, scale=SCALE,
                                     bias=nmx[:, h, 1:2], accum_out=rs[:, h, 1:2]).then_inc(exp_done, 1)

            def keep_probT(h):
                act.wait_ge(probT_ready, h + 1)
                nc.scalar.activation(qT[:, h, :], y[2 + h % 2][:, 0:SEQ], ACT.Copy)
                nc.scalar.activation(kT[:, h, 0:P], y[2 + h % 2][:, SEQ:384], ACT.Copy).then_inc(probT_kept, 1)

            for i in range(4):
                soft_exp(2 * i)
                split_hi(n + 8 + i + 2)
                soft_exp(2 * i + 1)
                act.wait_ge(w_used, n + 8 + i + 1)
                nc.scalar.activation(v_sb[:, :, 256 * i:256 * i + 256],
                                     gu[i % 2].rearrange("p (t n) -> p t n", t=2), ACT.Copy).then_inc(proj_kept, 1)
                keep_probT(2 * i)
                keep_probT(2 * i + 1)
            nc.scalar.preload_act_table(ACT.Sqrt)
            for h in range(4):
                keep_yT(0, h)
            keep_gate(1)
            split_hi(N_WO[0] + 2)
            keep_yT(0, 4)
            keep_yT(0, 5)
            split_hi(N_WO[0] + 3)
            keep_yT(0, 6)
            keep_yT(0, 7)
            split_hi(N_WO[0] + 4)
            split_hi(N_WO[0] + 5)
            norm(1, 2)
            nc.scalar.preload_act_table(ACT.Silu)
            ffn(1)
            norm(2, 3)
            n = N_KV
            for i in range(8):
                split_hi(n + i + 2)
                act.wait_ge(w_used, n + i + 1)
                if i < 4:
                    nc.scalar.activation(kT[:, 2 * i:2 * i + 2, :], gu[i % 2].rearrange("p (h t) -> p h t", h=2),
                                         ACT.Copy).then_inc(proj_kept, 1)
                else:
                    nc.scalar.activation(v_sb[:, :, 256 * (i - 4):256 * (i - 4) + 256],
                                         gu[i % 2].rearrange("p (t n) -> p t n", t=2), ACT.Copy)\
                      .then_inc(proj_kept, 1)
            nc.scalar.preload_act_table(ACT.Silu)
            h_tile(4, 0)
            h_tile(4, 1)
            ffn(2)
            norm(3, 5)
            nc.scalar.preload_act_table_set("natural_log_exp_and_others")
            n = N_Q

            def stick_logs(h):
                act.wait_ge(z_ready, h + 1)
                if h >= 2:
                    act.wait_ge(pv_ready, HEADS + h - 1)
                nc.scalar.activation(prob[:, h % 2, :], y[h % 4][:, 0:384], ACT.Abs).then_inc(abs_done, 1)
                act.wait_ge(abs_done, h + 1)
                nc.scalar.activation(prob[:, h % 2, :], prob[:, h % 2, :], ACT.Exp, scale=-1.0).then_inc(expn_done, 1)
                act.wait_ge(expn_done, h + 1)
                nc.scalar.activation(prob[:, h % 2, :], prob[:, h % 2, :], ACT.Ln, bias=1.0).then_inc(ln1p_done, 1)

            def stick_weights(h):
                act.wait_ge(stick_ready, h + 1)
                nc.scalar.activation(prob[:, h % 2, :], y[h % 4][:, 0:384], ACT.Exp).then_inc(weight_ready, 1)

            for i in range(4):
                split_hi(n + i + 2)
                act.wait_ge(w_used, n + i + 1)
                if i == 0:
                    act.wait_ge(x_ready, 2 * 3 + 2)
                nc.scalar.activation(qT[:, 2 * i:2 * i + 2, :], gu[i % 2].rearrange("p (h t) -> p h t", h=2),
                                     ACT.Copy, scale=SCALE).then_inc(proj_kept, 1)
            load_ln_rows(4)
            split_hi(N_WO[1] + 2)
            keep_gate(4)
            for h in range(HEADS + 2):
                if h < HEADS:
                    stick_logs(h)
                if 1 <= h <= HEADS:
                    stick_weights(h - 1)
                if h >= 2:
                    keep_yT(1, h - 2)
            nc.scalar.preload_act_table(ACT.Sqrt)
            for j in range(1, 4):
                split_hi(N_WO[1] + j + 2)
            norm(4, 6)
            nc.scalar.preload_act_table(ACT.Silu)
            ffn(3)
            norm(5, None)

        @block.vector
        def _(dve):
            steps = [0]

            def own(instruction):
                steps[0] += 1
                instruction.then_inc(dve_step, 1)
                dve.wait_ge(dve_step, steps[0])

            def split_lo(n, at=0):
                dve.wait_ge(w_hi_ready, n + at + 1)
                nc.vector.tensor_tensor(w_lo[:, n % SPL, :], raw[:, n % RAW, :], w_hi[:, n % SPL, :].bitcast(F32),
                                        ALU.subtract).then_inc(w_lo_ready, 1)

            def accumulate(u, q):
                dve.wait_ge(ada_in[q % 2], 32 * u + 16 * (q // 2) + 16)
                if q == 0:
                    dve.wait_ge(bias_in, 16 * u + 16)
                for r in range(2):
                    if not (isinstance(u, int) and u == 0 and q == 0 and r == 0):
                        dve.wait_ge(acc_steps, 8 * u + 2 * q + r)
                    nc.vector.scalar_tensor_tensor(out=acc[:, :], in0=ada[:, q % 2, r, :],
                                                   scalar=cond[:, 2 * q + r:2 * q + r + 1],
                                                   in1=bias0[:, :] if q == 0 and r == 0 else acc[:, :],
                                                   op0=ALU.mult, op1=ALU.add).then_inc(acc_steps, 1)

            def keep_unit(u):
                dve.wait_ge(unit_summed, u + 1)
                nc.vector.tensor_copy(modT[:, bass.ds(u, 1), :].rearrange("p a k -> p (a k)"), misc[0][:, 0:KT]).then_inc(mod_ready, 1)

            def coefficients(i):
                shift, scale, norm_i = H_OF[i]
                dve.wait_ge(mod_ready, scale + 1)
                a, b = coef[:, i, 0, :], coef[:, i, 1, :]
                if norm_i is None:
                    nc.vector.tensor_copy(b, modT[:, shift, :])
                    nc.vector.tensor_scalar_add(a, modT[:, scale, :], 1.0).then_inc(coef_ready, 1)
                    return
                g_t = lnT[:, 0, norm_i * KT:(norm_i + 1) * KT]
                b_t = lnT[:, 1, norm_i * KT:(norm_i + 1) * KT]
                own(nc.vector.scalar_tensor_tensor(out=b, in0=modT[:, scale, :], scalar=1.0, in1=b_t,
                                                   op0=ALU.add, op1=ALU.mult))
                own(nc.vector.tensor_tensor(b, b, modT[:, shift, :], ALU.add))
                nc.vector.scalar_tensor_tensor(out=a, in0=modT[:, scale, :], scalar=1.0, in1=g_t,
                                               op0=ALU.add, op1=ALU.mult).then_inc(coef_ready, 1)

            def gate_diagonals(i):
                dve.wait_ge(mod_ready, GATE_OF[i] + 1)
                for k in range(KT):
                    last = nc.vector.tensor_scalar(h_full[:, k, :], ident, modT[:, GATE_OF[i], k:k + 1], None, ALU.mult)
                last.then_inc(diag_ready, 1)

            def ffn_tile(f, s, t, turn=0):
                j = 2 * STEPS * f + 2 * s + t
                dve.wait_ge(silu_ready, j + 1 + 4 * turn)
                nc.vector.tensor_tensor(a_full[:, t, :], gu[t][:, SEQ:2 * SEQ], silu_t[:, t, :], ALU.mult)\
                  .then_inc(a_ready, 1)
                dve.wait_ge(a_hi_ready, j + 1 + 4 * turn)
                nc.vector.tensor_tensor(a_lo[:, s % 2, t, :], a_full[:, t, :], a_hi[:, s % 2, t, :].bitcast(F32),
                                        ALU.subtract).then_inc(a_lo_ready, 1)

            def ffn_step(f, n, s, splits=3, at=0, turn=0, u=None, parts=((), (), ())):
                for t in range(2):
                    ffn_tile(f, s, t, turn)
                    if t < splits:
                        split_lo(n + 3 * s + 2 + t, at)
                    for q in parts[t]:
                        accumulate(u, q)
                if splits == 3:
                    split_lo(n + 3 * s + 4, at)
                for q in parts[2]:
                    accumulate(u, q)

            def ffn(f, first_unit, before_gate):
                n = N_FFN[f]
                ffn_step(f, n, 0)
                last = f == 3
                with dve.Fori(0, STEPS // 2 - (1 if last else 0)) as b:
                    if first_unit is None:
                        for j in range(2):
                            ffn_step(f, n, 1 + j, at=6 * b, turn=b)
                    else:
                        u = b + first_unit
                        ffn_step(f, n, 1, at=6 * b, turn=b, u=u, parts=((0,), (1,), (2,)))
                        ffn_step(f, n, 2, at=6 * b, turn=b, u=u, parts=((3,), (), ()))
                        keep_unit(u)
                if last:
                    ffn_step(f, n, STEPS - 2)
                    ffn_step(f, n, STEPS - 1, splits=1)
                for i in before_gate:
                    coefficients(i)
                gate_diagonals(NORM_OF_FFN[f])

            def h_tile(i, t):
                dve.wait_ge(turned, 4 * i + 2 * t + 2)
                dve.wait_ge(coef_ready, i + 1)
                for k in range(KT // 2, KT):
                    last = nc.vector.tensor_scalar(h_fulls[t][:, k, :], tr_bank[t][1][:, (k - 4) * P:(k - 3) * P],
                                                   coef[:, i, 0, k:k + 1], coef[:, i, 1, k:k + 1], ALU.mult, ALU.add)
                last.then_inc(h_dve, 1)
                for half in range(2):
                    dve.wait_ge(h_hi_ready, 4 * i + 2 * t + half + 1)
                    nc.vector.tensor_tensor(hT_lo[:, 4 * half:4 * half + 4, t * P:(t + 1) * P],
                                            h_fulls[t][:, 4 * half:4 * half + 4, :],
                                            hT_hi[:, 4 * half:4 * half + 4, t * P:(t + 1) * P].bitcast(F32),
                                            ALU.subtract).then_inc(h_lo_ready, 1)

            def normalise(i, t):
                if t == 0:
                    dve.wait_ge(y_ready, i + 1)
                else:
                    dve.wait_ge(w_used, LAST_CHUNK[i] + 1)
                dve.wait_ge(gate_ready, i + 1)
                own(nc.vector.tensor_tensor(z[:, t, :], y_tok[t], gate[:, :], ALU.mult))
                own(nc.vector.scalar_tensor_tensor(out=z[:, t, :], in0=x_sb[:, t, :], scalar=ALPHA, in1=z[:, t, :],
                                                   op0=ALU.mult, op1=ALU.add))
                nc.vector.bn_stats(stats[:, t, 0, :], z[:, t, 0:512])
                own(nc.vector.bn_stats(stats[:, t, 1, :], z[:, t, 512:1024]))
                nc.vector.bn_aggr(mv[:, t, :], stats[:, t, :, :].rearrange("p a b -> p (a b)")).then_inc(var_ready, 1)
                dve.wait_ge(sd_ready, 2 * i + t + 1)
                own(nc.vector.reciprocal(rstd[:, t:t + 1], sd[:, t:t + 1]))
                nc.vector.tensor_scalar(z[:, t, :], z[:, t, :], mv[:, t, 0:1], rstd[:, t:t + 1],
                                        ALU.subtract, ALU.mult).then_inc(xn_ready, 1)

            def new_x(i, t):
                dve.wait_ge(ln_row_in, 32 * (i + 1))
                dve.wait_ge(xn_ready, 2 * i + t + 1)
                own(nc.vector.tensor_tensor(x_sb[:, t, :], z[:, t, :], g_row[:, :], ALU.mult))
                nc.vector.tensor_tensor(x_sb[:, t, :], x_sb[:, t, :], b_row[:, :], ALU.add).then_inc(x_ready, 1)

            def norm(i, h):
                for t in range(TT):
                    normalise(i, t)
                    if h is not None:
                        h_tile(h, t)
                    else:
                        new_x(i, t)
                if h is not None:
                    for t in range(TT):
                        new_x(i, t)

            def keep_yT(layer, h):
                dve.wait_ge(yT_hi_ready, HEADS * layer + h + 1)
                nc.vector.tensor_tensor(hT_lo[:, h, :], gu[h % 2][:, 0:SEQ], hT_hi[:, h, :].bitcast(F32),
                                        ALU.subtract).then_inc(yT_lo_ready, 1)

            nc.vector.memset(eps_t[:, :], EPS)
            nc.vector.memset(all_ones[:, :], 1.0)
            nc.vector.memset(neg_ones[:, :], -1.0)
            nc.vector.memset(zeros[:, :], 0.0)
            nc.vector.memset(bias0[:, :], 0.0).then_inc(set_up, 1)
            dve.wait_ge(cond_ready, 1)
            for q in range(4):
                accumulate(0, q)
            keep_unit(0)
            for q in range(4):
                accumulate(1, q)
            keep_unit(1)
            coefficients(0)
            dve.wait_ge(x_in, 32)
            split_lo(0)
            h_tile(0, 0)
            h_tile(0, 1)
            split_lo(1)
            ffn(0, unit(0, 2), (1,))
            norm(0, 1)
            n = N_QKV

            def rope(i):
                side = (qT, kT)[i // 4][0:ROT, 2 * (i % 4):2 * (i % 4) + 2, :]
                two = [ROT, 2, SEQ]
                dve.wait_ge(rot_ready, i + 1)
                if i:
                    dve.wait_ge(rope_done, i)
                own(nc.vector.tensor_tensor(rope_t.rearrange("p (h t) -> p h t", h=2),
                                            misc[i % 2][0:ROT, :].rearrange("p (h t) -> p h t", h=2),
                                            sin_t.unsqueeze(1).to_broadcast(two), ALU.mult))
                own(nc.vector.tensor_tensor(side, side, cos_t.unsqueeze(1).to_broadcast(two), ALU.mult))
                nc.vector.tensor_tensor(side, side, rope_t.rearrange("p (h t) -> p h t", h=2), ALU.add)\
                  .then_inc(rope_done, 1)

            for i in range(8):
                split_lo(n + i + 2)
                if i >= 1:
                    rope(i - 1)
                if i < 4:
                    accumulate(unit(0, 7), i)
            rope(7)

            def soft_max(h):
                dve.wait_ge(score_ready, h + 1)
                nc.vector.reduce_max(mx[:, h, 0:1], y[h % 2][:, 0:P], AX.X)
                own(nc.vector.reduce_max(mx[:, h, 1:2], y[h % 2][:, P:384], AX.X))
                nc.vector.tensor_scalar(nmx[:, h, :], mx[:, h, :], -SCALE, None, ALU.mult).then_inc(nmax_ready, 1)

            def soft_scale(h):
                dve.wait_ge(exp_done, h + 1)
                own(nc.vector.reciprocal(rinv[:, h, :], rs[:, h, :]))
                nc.vector.tensor_scalar(prob[:, h % 2, 0:P], prob[:, h % 2, 0:P], rinv[:, h, 0:1], None, ALU.mult)
                nc.vector.tensor_scalar(prob[:, h % 2, P:384], prob[:, h % 2, P:384], rinv[:, h, 1:2], None,
                                        ALU.mult).then_inc(prob_ready, 1)

            for i in range(4):
                soft_max(2 * i)
                soft_max(2 * i + 1)
                soft_scale(2 * i)
                split_lo(n + 8 + i + 2)
                soft_scale(2 * i + 1)
            keep_unit(unit(0, 7))
            coefficients(2)
            gate_diagonals(1)
            for h in range(4):
                keep_yT(0, h)
            split_lo(N_WO[0] + 2)
            keep_yT(0, 4)
            keep_yT(0, 5)
            split_lo(N_WO[0] + 3)
            keep_yT(0, 6)
            keep_yT(0, 7)
            split_lo(N_WO[0] + 4)
            split_lo(N_WO[0] + 5)
            norm(1, 2)
            ffn(1, unit(0, 8), (3, 4))
            norm(2, 3)
            for i in range(8):
                split_lo(N_KV + i + 2)
            h_tile(4, 0)
            h_tile(4, 1)
            ffn(2, unit(1, 2), (5,))
            norm(3, 5)
            for i in range(4):
                split_lo(N_Q + i + 2)
                accumulate(unit(1, 7), i)
            keep_unit(unit(1, 7))
            coefficients(6)
            gate_diagonals(4)
            split_lo(N_WO[1] + 2)

            def stick_sums(h):
                dve.wait_ge(ln1p_done, h + 1)
                own(nc.vector.scalar_tensor_tensor(out=sp_t[:, h % 2, :], in0=y[h % 4][:, 0:384], scalar=0.0,
                                                   in1=prob[:, h % 2, :], op0=ALU.max, op1=ALU.add))
                nc.vector.tensor_tensor(sp_t[:, h % 2, 0:P], sp_t[:, h % 2, 0:P], keep, ALU.mult)
                nc.vector.tensor_tensor(sp_t[:, h % 2, SEQ:384], sp_t[:, h % 2, SEQ:384], keep, ALU.mult)\
                  .then_inc(keepsum_ready, 1)

            for h in range(HEADS + 2):
                if h < HEADS:
                    stick_sums(h)
                    if h % 2 == 1:
                        accumulate(unit(1, 8), h // 2)
                if h >= 2:
                    keep_yT(1, h - 2)
            keep_unit(unit(1, 8))
            for j in range(1, 4):
                split_lo(N_WO[1] + j + 2)
            norm(4, 6)
            ffn(3, None, ())
            norm(5, None)

        @block.tensor
        def _(pe):
            def three(dst, stat, mov, start, stop):
                (s_hi, s_lo), (m_hi, m_lo) = stat, mov
                nc.tensor.matmul(dst, s_hi, m_hi, start=start, stop=False)
                nc.tensor.matmul(dst, s_hi, m_lo, start=False, stop=False)
                return nc.tensor.matmul(dst, s_lo, m_hi, start=False, stop=stop)

            def w_cols(n, k, c0, width):
                at = k * 256 + c0
                return w_hi[:, n % SPL, at:at + width], w_lo[:, n % SPL, at:at + width]

            def w_rows(n, j, half):
                at = j * 1024 + half * 512
                return w_hi[:, n % SPL, at:at + 512], w_lo[:, n % SPL, at:at + 512]

            def h_all(k):
                return hT_hi[:, k, :], hT_lo[:, k, :]

            def h_tok(k, t):
                return hT_hi[:, k, t * P:(t + 1) * P], hT_lo[:, k, t * P:(t + 1) * P]

            def turn_tiles(src, wait):
                for t in range(TT):
                    wait(t)
                    for k in range(KT):
                        last = nc.tensor.transpose(tr_bank[t][k // 4][:, (k % 4) * P:(k % 4 + 1) * P],
                                                   src[:, t, k * P:(k + 1) * P], ident)
                        if k % 4 == 3:
                            last.then_inc(turned, 1)

            def sum_unit(u):
                pe.wait_ge(acc_steps, 8 * u + 8)
                for k in range(KT):
                    last = nc.tensor.matmul(misc[0][:, k:k + 1], acc[:, k * P:(k + 1) * P], all_ones[:, 0:1],
                                            start=True, stop=True)
                last.then_inc(unit_summed, 1)

            def spread_gate(i):
                pe.wait_ge(diag_ready, i + 1)
                for k in range(KT):
                    last = nc.tensor.matmul(misc[k // 4][:, (k % 4) * P:(k % 4 + 1) * P], all_ones[:, :],
                                            h_full[:, k, :], start=True, stop=True)
                last.then_inc(gate_spread, 1)

            def columns_out(n, dst, at=0):
                pe.wait_ge(w_lo_ready, n + at + 1)
                for j in range(2):
                    for k in range(KT):
                        last = three(dst[:, j * SEQ:(j + 1) * SEQ], w_cols(n, k, j * P, P), h_all(k),
                                     k == 0, k == KT - 1)
                last.then_inc(w_used, 1)

            def tokens_out(n, dst):
                pe.wait_ge(w_lo_ready, n + 1)
                for t in range(TT):
                    for k in range(KT):
                        last = three(dst[:, t * 256:(t + 1) * 256], h_tok(k, t), w_cols(n, k, 0, 256),
                                     k == 0, k == KT - 1)
                last.then_inc(w_used, 1)

            def add_rows(n, operand, first, done=None, at=0):
                pe.wait_ge(w_lo_ready, n + at + 1)
                for t in range(TT):
                    for j in range(2):
                        hi, lo = operand(j, t)
                        for half in range(2):
                            m = w_rows(n, j, half)
                            dst = y[2 * t + half]
                            st, en = first and j == 0, bool(done) and j == 1
                            nc.tensor.matmul(dst, hi, m[0], start=st, stop=False)
                            nc.tensor.matmul(dst, hi, m[1], start=False, stop=False)
                            last = nc.tensor.matmul(dst, lo, m[0], start=False, stop=en)
                    if done and t == 0:
                        last.then_inc(y_ready, 1)
                last.then_inc(w_used, 1)

            def in_tile(f, n, s, t, at=0, turn=0):
                j = 2 * STEPS * f + 2 * s + t
                g, u = (n, n + 1) if s == 0 else (n + 3 * s - 1, n + 3 * s)
                if j >= 2:
                    pe.wait_ge(a_ready, j - 1 + 4 * turn)
                for part, m in enumerate((g, u)):
                    if t == 0:
                        pe.wait_ge(w_lo_ready, m + at + 1)
                    for k in range(KT):
                        last = three(gu[t][:, part * SEQ:(part + 1) * SEQ], w_cols(m, k, t * P, P), h_all(k),
                                     k == 0, k == KT - 1)
                    if t == 1:
                        last.then_inc(w_used, 1)
                if t == 0:
                    last.then_inc(gu_ready, 1)

            def ffn_out(f, n, s, first=False, done=None, at=0, turn=0):
                pe.wait_ge(a_lo_ready, 2 * STEPS * f + 2 * s + 2 + 4 * turn)
                m = n + 3 * s + 4 if s < STEPS - 1 else n + FFN_CHUNKS - 1
                add_rows(m, lambda j, t: (a_hi[:, s % 2, j, t * P:(t + 1) * P], a_lo[:, s % 2, j, t * P:(t + 1) * P]),
                         first, done, at)

            def ffn(f, first_unit):
                n = N_FFN[f]
                pe.wait_ge(h_lo_ready, 4 * H_OF_FFN[f] + 4)
                for t in range(2):
                    in_tile(f, n, 0, t)
                for i in range(4):
                    nc.tensor.matmul(y[i], zeros[:, 0:P], zeros[:, :], start=True, stop=False)
                with pe.Fori(0, STEPS // 2) as b:
                    for s in (1, 2):
                        for t in range(2):
                            in_tile(f, n, s, t, at=6 * b, turn=b)
                        ffn_out(f, n, s - 1, at=6 * b, turn=b)
                    if first_unit is not None:
                        sum_unit(b + first_unit)
                spread_gate(NORM_OF_FFN[f])
                ffn_out(f, n, STEPS - 1, done=True)

            def norm(i):
                turn_tiles(z, lambda t: pe.wait_ge(xn_ready, 2 * i + t + 1))

            def weigh_values(layer, h, first, second):
                if h >= 2:
                    pe.wait_ge(yT_lo_ready, HEADS * layer + h - 1)
                nc.tensor.matmul(gu[h % 2][:, 0:SEQ], v_sb[:, 0, h * DH:(h + 1) * DH], first, start=True, stop=False)
                nc.tensor.matmul(gu[h % 2][:, P:SEQ], v_sb[:, 1, h * DH:(h + 1) * DH], second, start=False, stop=True)\
                  .then_inc(pv_ready, 1)

            def output_rows(layer, j):
                pe.wait_ge(yT_lo_ready, HEADS * layer + 2 * j + 2)
                add_rows(N_WO[layer] + j, lambda jj, t: h_tok(2 * j + jj, t), j == 0, j == 3)

            pe.wait_ge(set_up, 1)
            pe.wait_ge(cst_in, 16)
            pe.wait_ge(lnT_in, 32)
            for r in range(2):
                last = nc.tensor.transpose(misc[1][:, 48 * r:48 * r + 48], tmp[0:48, r * P:(r + 1) * P],
                                           ident[0:48, 0:48])
            last.then_inc(lnT_turned, 1)
            sum_unit(0)
            pe.wait_ge(mod_ready, 1)
            sum_unit(1)
            pe.wait_ge(x_in, 32)
            pe.wait_ge(mod_ready, 2)
            pe.wait_ge(lnT_ready, 1)
            turn_tiles(x_sb, lambda t: None)
            ffn(0, unit(0, 2))
            norm(0)
            pe.wait_ge(h_lo_ready, 8)

            def rotate(i):
                pe.wait_ge(proj_kept, i + 1)
                if i >= 2:
                    pe.wait_ge(rope_done, i - 1)
                nc.tensor.matmul(misc[i % 2], rot_m,
                                 (qT, kT)[i // 4][0:ROT, 2 * (i % 4):2 * (i % 4) + 2, :].rearrange("p h t -> p (h t)"),
                                 start=True, stop=True).then_inc(rot_ready, 1)

            for i in range(8):
                if i >= 2:
                    pe.wait_ge(proj_kept, i - 1)
                columns_out(N_QKV + i, gu[i % 2])
                if i:
                    rotate(i - 1)
            rotate(7)

            def scores(h):
                if h >= 2:
                    pe.wait_ge(exp_done, h - 1)
                s = y[h % 2]
                nc.tensor.matmul(s[:, 0:P], qT[:, h, 0:P], kT[:, h, 0:P], start=True, stop=False)
                nc.tensor.matmul(s[:, 0:P], ident, causal, start=False, stop=True)
                nc.tensor.matmul(s[:, P:384], qT[:, h, P:SEQ], kT[:, h, :], start=True, stop=False)
                nc.tensor.matmul(s[:, SEQ:384], ident, causal, start=False, stop=True).then_inc(score_ready, 1)

            def turn_probs(h):
                pe.wait_ge(prob_ready, h + 1)
                if h >= 2:
                    pe.wait_ge(probT_kept, h - 1)
                for b in range(3):
                    last = nc.tensor.transpose(y[2 + h % 2][:, b * P:(b + 1) * P], prob[:, h % 2, b * P:(b + 1) * P],
                                               ident)
                last.then_inc(probT_ready, 1)

            pe.wait_ge(rope_done, 8)
            for i in range(4):
                scores(2 * i)
                scores(2 * i + 1)
                pe.wait_ge(proj_kept, 8 + i - 1)
                tokens_out(N_QKV + 8 + i, gu[i % 2])
                if i == 0:
                    sum_unit(unit(0, 7))
                turn_probs(2 * i)
                turn_probs(2 * i + 1)
            pe.wait_ge(proj_kept, 12)
            pe.wait_ge(probT_kept, HEADS)
            for h in range(4):
                weigh_values(0, h, qT[:, h, :], kT[:, h, 0:P])
            spread_gate(1)
            for j in range(4):
                output_rows(0, j)
                if j < 2:
                    for h in (2 * j + 4, 2 * j + 5):
                        weigh_values(0, h, qT[:, h, :], kT[:, h, 0:P])
            norm(1)
            ffn(1, unit(0, 8))
            norm(2)
            pe.wait_ge(h_lo_ready, 4 * 3 + 4)
            for i in range(8):
                if i >= 2:
                    pe.wait_ge(proj_kept, 12 + i - 1)
                if i < 4:
                    columns_out(N_KV + i, gu[i % 2])
                else:
                    tokens_out(N_KV + i, gu[i % 2])
            pe.wait_ge(x_ready, 2 * 2 + 2)
            pe.wait_ge(proj_kept, 20)
            turn_tiles(x_sb, lambda t: None)
            ffn(2, unit(1, 2))
            norm(3)
            pe.wait_ge(h_lo_ready, 4 * 5 + 4)
            for i in range(4):
                if i >= 2:
                    pe.wait_ge(proj_kept, 20 + i - 1)
                columns_out(N_Q + i, gu[i % 2])
            sum_unit(unit(1, 7))
            spread_gate(4)
            pe.wait_ge(proj_kept, 24)

            def stick_scores(h):
                s = y[h % 4]
                nc.tensor.matmul(s[:, 0:SEQ], kT[:, h, 0:P], qT[:, h, :], start=True, stop=True)
                nc.tensor.matmul(s[:, SEQ:384], kT[:, h, P:SEQ], qT[:, h, P:SEQ], start=False, stop=True,
                                 skip_group_check=True).then_inc(z_ready, 1)

            def stick_log_weights(h):
                pe.wait_ge(keepsum_ready, h + 1)
                s, first, second = y[h % 4], sp_t[:, h % 2, 0:SEQ], sp_t[:, h % 2, SEQ:384]
                for dst, stat, mov in ((s[:, 0:SEQ], tri, first), (s[:, P:SEQ], neg_ones[:, :], second),
                                       (s[:, SEQ:384], tri, second), (s[:, 0:P], ident, strict),
                                       (s[:, SEQ:384], ident, strict)):
                    last = nc.tensor.matmul(dst, stat, mov, start=False, stop=True, skip_group_check=True)
                last.then_inc(stick_ready, 1)

            for h in range(HEADS + 2):
                if h < HEADS:
                    stick_scores(h)
                if h >= 2:
                    pe.wait_ge(weight_ready, h - 1)
                    weigh_values(1, h - 2, prob[:, h % 2, 0:SEQ], prob[:, h % 2, SEQ:384])
                if 1 <= h <= HEADS:
                    stick_log_weights(h - 1)
            sum_unit(unit(1, 8))
            for j in range(4):
                output_rows(1, j)
            norm(4)
            ffn(3, None)


_INS = ["x", "c", "w_ada", "b_ada", "ln_g", "ln_b", "w_ffn_in", "w_ffn_out", "w_qkv_a", "w_q_b",
        "w_kv_ada", "b_kv_ada", "w_kv_b", "w_o"]


def shape_constants():
    row, col = np.arange(P)[:, None], np.arange(P)[None, :]
    a = np.zeros((P, C_ALL), np.float32)
    a[:, C_ID:C_ID + P] = row == col
    a[:, C_TRI:C_TRI + P] = np.where(row >= col, -1.0, 0.0)
    a[:, C_CAUSAL:C_CAUSAL + P] = np.where(col > row, -1e30, 0.0)
    a[:, C_STRICT:C_STRICT + P] = np.where(row >= col, -1e30, 0.0)
    a[:, C_KEEP:C_KEEP + P] = row < col
    half = ROT // 2
    freq = np.power(np.float32(500000.0), -np.arange(half, dtype=np.float32) * np.float32(2.0) / np.float32(ROT))
    angle = np.arange(SEQ, dtype=np.float32)[None, :] * freq.astype(np.float32)[:, None]
    for i in range(2):
        a[i * half:(i + 1) * half, C_COS:C_COS + SEQ] = np.cos(angle)
        a[i * half:(i + 1) * half, C_SIN:C_SIN + SEQ] = np.sin(angle)
    for i in range(half):
        a[i + half, C_ROT + i] = -1.0
        a[i, C_ROT + i + half] = 1.0
    return a


def kernel(**inputs):
    import concourse.bacc as bacc
    from concourse.bass_utils import run_bass_kernel_spmd

    nc = bacc.Bacc("TRN2", target_bir_lowering=False, num_devices=1)
    arrays, args = {}, []
    for name in _INS:
        a = np.ascontiguousarray(inputs[name])
        arrays["in_" + name] = a
        args.append(nc.dram_tensor("in_" + name, a.shape, mybir.dt.from_np(a.dtype), kind="ExternalInput").ap())
    arrays["in_consts"] = shape_constants()
    args.append(nc.dram_tensor("in_consts", (P, C_ALL), F32, kind="ExternalInput").ap())
    args.append(nc.dram_tensor("out", (1, SEQ, D), F32, kind="ExternalOutput").ap())
    build(nc, *args)
    r = run_bass_kernel_spmd(nc, [arrays], core_ids=[0])
    return r.results[0]["out"]
```

```python
import math
from contextlib import ExitStack

import numpy as np

import concourse.bass as bass
from concourse import mybir

F32 = mybir.dt.float32
F32R = mybir.dt.float32r
ACT = mybir.ActivationFunctionType
ALU = mybir.AluOpType
AX = mybir.AxisListType

P = 128
D = 1024
SEQ = 256
KT = D // P
TT = SEQ // P
HEADS = 8
DH = D // HEADS
ROT = DH // 4
DFF = 2816
STEPS = DFF // 256
LOOPS = (STEPS - 3) // 2
DEPTH = 2
ALPHA = (2.0 * DEPTH) ** 0.25
EPS = 1e-5
SCALE = DH ** -0.5
CH = 2048
RAW = 6
STAGED = 8
SPL = 3
MODS = 9

FFN_CHUNKS = 3 * STEPS
N_FFN = [0] * 4
N_FFN[0] = 0
N_QKV = N_FFN[0] + FFN_CHUNKS
N_WO = [N_QKV + 12, 0]
N_FFN[1] = N_WO[0] + 4
N_KV = N_FFN[1] + FFN_CHUNKS
N_FFN[2] = N_KV + 8
N_Q = N_FFN[2] + FFN_CHUNKS
N_WO[1] = N_Q + 4
N_FFN[3] = N_WO[1] + 4
N_ALL = N_FFN[3] + FFN_CHUNKS

U_KV = MODS
U_L = [0, MODS + 2]
UNITS = 2 * MODS + 2


def unit(layer, j):
    return U_L[layer] + j


H_OF = [(unit(0, 0), unit(0, 1), None),
        (unit(0, 3), unit(0, 4), 0),
        (unit(0, 6), unit(0, 7), 1),
        (U_KV, U_KV + 1, 2),
        (unit(1, 0), unit(1, 1), None),
        (unit(1, 3), unit(1, 4), 3),
        (unit(1, 6), unit(1, 7), 4)]
GATE_OF = [unit(0, 2), unit(0, 5), unit(0, 8), unit(1, 2), unit(1, 5), unit(1, 8)]
GATE_W = [0.5, 1.0, 0.5, 0.5, 1.0, 0.5]
C_ID, C_TRI, C_CAUSAL, C_STRICT, C_KEEP, C_COS, C_SIN, C_ROT = (
    0, 128, 256, 384, 512, 640, 896, 1152)
C_ALL = 1280
NORM_OF_FFN = [0, 2, 3, 5]
LAST_CHUNK = [N_FFN[0] + FFN_CHUNKS - 1, N_WO[0] + 3, N_FFN[1] + FFN_CHUNKS - 1,
              N_FFN[2] + FFN_CHUNKS - 1, N_WO[1] + 3, N_FFN[3] + FFN_CHUNKS - 1]
H_OF_FFN = [0, 2, 4, 6]


def build(nc, x, c, w_ada, b_ada, ln_g, ln_b, w_ffn_in, w_ffn_out, w_qkv_a, w_q_b,
          w_kv_ada, b_kv_ada, w_kv_b, w_o, consts, out):
    ctx = ExitStack()
    with ctx:
        def sb(name, shape, dt=F32):
            return ctx.enter_context(nc.sbuf_tensor(name, shape, dt))

        def sem(name):
            return ctx.enter_context(nc.semaphore(name))

        raw = sb("raw", [P, RAW, CH])
        w_hi = sb("w_hi", [P, SPL, CH], F32R)
        w_lo = sb("w_lo", [P, SPL, CH], F32R)
        ada = sb("ada", [P, 2, 2, 1024])
        acc = sb("acc", [P, 1024])
        bias0 = sb("bias0", [P, 1024])
        x_sb = sb("x_sb", [P, TT, D])
        hT_hi = sb("hT_hi", [P, KT, SEQ], F32R)
        hT_lo = sb("hT_lo", [P, KT, SEQ], F32R)
        a_hi = sb("a_hi", [P, 2, 2, SEQ], F32R)
        a_lo = sb("a_lo", [P, 2, 2, SEQ], F32R)
        tmp = sb("tmp", [P, 1536])
        h_full = sb("h_full", [P, KT, P])
        gate = sb("gate", [P, D])
        g_row = sb("g_row", [P, D])
        b_row = sb("b_row", [P, D])
        qT = sb("qT", [P, HEADS, SEQ])
        kT = sb("kT", [P, HEADS, SEQ])
        v_sb = sb("v_sb", [P, TT, D])
        cst = sb("cst", [P, C_ALL])
        modT = sb("modT", [P, UNITS, KT])
        coef = sb("coef", [P, len(H_OF), 2, KT])
        lnT = sb("lnT", [P, 2, 48])
        cond = sb("cond", [P, 8])
        total = sb("total", [P, TT])
        nmean = sb("nmean", [P, TT])
        sq = sb("sq", [P, TT])
        sd = sb("sd", [P, TT])
        rstd = sb("rstd", [P, TT])
        all_ones = sb("all_ones", [P, P])
        neg_ones = sb("neg_ones", [P, P])
        zeros = sb("zeros", [P, 512], mybir.dt.bfloat16)
        eps_t = sb("eps_t", [P, 1])
        mx = sb("mx", [P, HEADS, 2])
        nmx = sb("nmx", [P, HEADS, 2])
        rs = sb("rs", [P, HEADS, 2])
        rinv = sb("rinv", [P, HEADS, 2])

        ident = cst[:, C_ID:C_ID + P]
        tri = cst[:, C_TRI:C_TRI + P]
        causal = cst[:, C_CAUSAL:C_CAUSAL + P]
        strict = cst[:, C_STRICT:C_STRICT + P]
        keep = cst[:, C_KEEP:C_KEEP + P]
        cos_t = cst[0:ROT, C_COS:C_COS + SEQ]
        sin_t = cst[0:ROT, C_SIN:C_SIN + SEQ]
        rot_m = cst[0:ROT, C_ROT:C_ROT + P]
        silu_t = tmp[:, 0:512].rearrange("p (j t) -> p j t", j=2)
        a_full = tmp[:, 512:1024].rearrange("p (j t) -> p j t", j=2)
        prob = tmp[:, 0:768].rearrange("p (j t) -> p j t", j=2)
        sp_t = tmp[:, 768:1536].rearrange("p (j t) -> p j t", j=2)
        rope_t = tmp[0:ROT, 1024:1536]
        z = qT[:, :, :].rearrange("p (t h) s -> p t (h s)", t=TT)
        h_fulls = [h_full[:, :, :], tmp[:, 0:1024].rearrange("p (k t) -> p k t", k=KT)]

        psum = ctx.enter_context(nc.psum_tensor("psum", [P, 8, 512], F32))
        gu = [psum[:, 0, :], psum[:, 1, :]]
        misc = [psum[:, 2, :], psum[:, 3, :]]
        misc2 = psum[:, 2:4, :].rearrange("p b n -> p (b n)")
        y = [psum[:, 4 + i, :] for i in range(4)]
        y_tok = [psum[:, 4 + 2 * t:6 + 2 * t, :].rearrange("p b n -> p (b n)") for t in range(TT)]
        tr_bank = [misc, y[0:2]]

        raw_in = [sem(f"raw_in{i}") for i in range(RAW)]
        w_hi_ready = sem("w_hi_ready")
        w_lo_ready = sem("w_lo_ready")
        w_used = sem("w_used")
        ada_in = [sem(f"ada_in{i}") for i in range(2)]
        staged_in = [sem(f"staged_in{i}") for i in range(2)]
        bias_in = sem("bias_in")
        acc_steps = sem("acc_steps")
        unit_turned = sem("unit_turned")
        mod_ready = sem("mod_ready")
        cst_in = sem("cst_in")
        x_in = sem("x_in")
        c_in = sem("c_in")
        lnT_in = sem("lnT_in")
        set_up = sem("set_up")
        cond_ready = sem("cond_ready")
        lnT_turned = sem("lnT_turned")
        lnT_ready = sem("lnT_ready")
        ln_row_in = sem("ln_row_in")
        turned = sem("turned")
        h_act = sem("h_act")
        h_dve = sem("h_dve")
        h_hi_ready = sem("h_hi_ready")
        h_lo_ready = sem("h_lo_ready")
        coef_ready = sem("coef_ready")
        silu_ready = sem("silu_ready")
        a_ready = sem("a_ready")
        a_hi_ready = sem("a_hi_ready")
        a_lo_ready = sem("a_lo_ready")
        diag_ready = sem("diag_ready")
        gate_spread = sem("gate_spread")
        gate_ready = sem("gate_ready")
        y_ready = sem("y_ready")
        dve_step = sem("dve_step")
        mean_ready = sem("mean_ready")
        sq_ready = sem("sq_ready")
        sd_ready = sem("sd_ready")
        xn_ready = sem("xn_ready")
        x_ready = sem("x_ready")
        out_done = sem("out_done")
        proj_kept = sem("proj_kept")
        rot_ready = sem("rot_ready")
        rope_done = sem("rope_done")
        score_ready = sem("score_ready")
        nmax_ready = sem("nmax_ready")
        exp_done = sem("exp_done")
        prob_ready = sem("prob_ready")
        probT_ready = sem("probT_ready")
        probT_kept = sem("probT_kept")
        pv_ready = sem("pv_ready")
        yT_hi_ready = sem("yT_hi_ready")
        yT_lo_ready = sem("yT_lo_ready")
        z_ready = sem("z_ready")
        abs_done = sem("abs_done")
        expn_done = sem("expn_done")
        ln1p_done = sem("ln1p_done")
        keepsum_ready = sem("keepsum_ready")
        stick_ready = sem("stick_ready")
        weight_ready = sem("weight_ready")

        block = ctx.enter_context(nc.Block())

        def rows_by_tile(w):
            return w.rearrange("(k p) n -> p k n", p=P)

        def ada_view(w):
            return w.rearrange("(p k) n -> p k n", k=8)

        def columns_chunk(w, start):
            return [rows_by_tile(w)[:, half * 4:half * 4 + 4, bass.ds(start, 256)] for half in range(2)]

        def inner_chunk(w, start):
            return [rows_by_tile(w)[:, :, bass.ds(start + half * DFF, P)] for half in range(2)]

        def rows_chunk(w, start):
            return [rows_by_tile(w[bass.ds(start + half * P, P), :]) for half in range(2)]

        def staged(m):
            if m < RAW:
                return raw[:, m, :].rearrange("p (k n) -> p k n", k=2), raw_in[m]
            return ada[:, m % 2, :, :], staged_in[m % 2]

        PROJ = ([(N_QKV + i, w_qkv_a[0], 256 * i) for i in range(12)],
                [(N_KV + i, w_kv_b, 256 * i) for i in range(8)],
                [(N_Q + i, w_q_b[0], 256 * i) for i in range(4)])

        @block.sync
        def _(sp):
            def load(n, halves, at=None):
                if at is not None or n >= RAW:
                    sp.wait_ge(w_lo_ready, n - RAW + 1 if at is None else at + (n - RAW + 1))
                else:
                    sp.wait_ge(acc_steps, 2 * n + 2)
                for half, src in enumerate(halves):
                    dst = raw[:, n % RAW, half * (CH // 2):(half + 1) * (CH // 2)]
                    sp.dma_start(dst.rearrange("p (k n) -> p k n", n=src.shape[2]), src).then_inc(raw_in[n % RAW], 16)

            def load_step(w_in, w_out, n, s, b=None):
                at, c = (None, 0) if b is None else (6 * b, 512 * b)
                load(n + 3 * s - 1, inner_chunk(w_in, c + 256 * s), at)
                load(n + 3 * s, inner_chunk(w_in, c + (256 * s + P)), at)
                load(n + 3 * s + 1, rows_chunk(w_out, c + 256 * (s - 1)), at)

            def load_ffn(f):
                w_in, w_out, n = w_ffn_in[f // 2, f % 2], w_ffn_out[f // 2, f % 2], N_FFN[f]
                load(n, inner_chunk(w_in, 0))
                load(n + 1, inner_chunk(w_in, P))
                peeled = 2 if f == 0 else 0
                for s in range(1, 1 + peeled):
                    load_step(w_in, w_out, n, s)
                with sp.Fori(0, (STEPS - 1 - peeled) // 2) as b:
                    for s in (1 + peeled, 2 + peeled):
                        load_step(w_in, w_out, n, s, b)
                load(n + FFN_CHUNKS - 1, rows_chunk(w_out, DFF - 256))

            def load_wo(layer):
                for j in range(4):
                    load(N_WO[layer] + j, rows_chunk(w_o[layer], 256 * j))

            for m in range(STAGED):
                dst, landed = staged(m)
                sp.dma_start(dst, ada_view(w_ada[0])[:, 2 * (m % 4):2 * (m % 4) + 2,
                                                     1024 * (m // 4):1024 * (m // 4 + 1)]).then_inc(landed, 16)
                if m == 3:
                    sp.dma_start(cst[:, :], consts).then_inc(cst_in, 16)
                    for t in range(TT):
                        sp.dma_start(x_sb[:, t, :], x[0, t * P:(t + 1) * P, :]).then_inc(x_in, 16)
            load_ffn(0)
            for n, w, at in PROJ[0]:
                load(n, columns_chunk(w, at))
            load_wo(0)
            load_ffn(1)
            for n, w, at in PROJ[1]:
                load(n, columns_chunk(w, at))
            load_ffn(2)
            for n, w, at in PROJ[2]:
                load(n, columns_chunk(w, at))
            load_wo(1)
            load_ffn(3)
            for t in range(TT):
                sp.wait_ge(x_ready, 2 * 5 + t + 1)
                sp.dma_start(out[0, t * P:(t + 1) * P, :], x_sb[:, t, :]).then_inc(out_done, 16)
            sp.wait_ge(out_done, 32)

        @block.gpsimd
        def _(pool):
            def load_unit(w, b, j, u):
                if u:
                    pool.wait_ge(acc_steps, 8 * u - 7)
                pool.dma_start(bias0[0:1, :], b[j * 1024:(j + 1) * 1024].rearrange("(a n) -> a n", a=1))\
                    .then_inc(bias_in, 16)
                for q in range(4 if 4 * u >= STAGED else 0):
                    pool.wait_ge(acc_steps, 8 * u + 2 * q - 2)
                    pool.dma_start(ada[:, q % 2, :, :],
                                   ada_view(w)[:, 2 * q:2 * q + 2, j * 1024:(j + 1) * 1024])\
                        .then_inc(ada_in[q % 2], 16)

            pool.wait_ge(set_up, 1)
            for j in range(MODS):
                load_unit(w_ada[0], b_ada[0], j, j)
            for j in range(2):
                load_unit(w_kv_ada, b_kv_ada, j, j + U_KV)
            for j in range(MODS):
                load_unit(w_ada[1], b_ada[1], j, j + U_L[1])

        @block.scalar
        def _(act):
            def split_hi(n, at=0, turn=0):
                act.wait_ge(raw_in[n % RAW], 32 * (n // RAW + 1) + 16 + 32 * turn)
                if n >= SPL:
                    act.wait_ge(w_used, n + at - SPL + 1)
                nc.scalar.activation(w_hi[:, n % SPL, :], raw[:, n % RAW, :], ACT.Copy).then_inc(w_hi_ready, 1)

            def silu(f, n, s, t, at=0):
                act.wait_ge(w_used, (n + 3 * s - 1 if s else n) + t + 1 + at)
                nc.scalar.activation(silu_t[:, t, :], gu[t][:, 0:SEQ], ACT.Silu).then_inc(silu_ready, 1)

            def inner_hi(f, s, t, turn=0):
                act.wait_ge(a_ready, 2 * STEPS * f + 2 * s + t + 1 + 4 * turn)
                nc.scalar.activation(a_hi[:, s % 2, t, :], a_full[:, t, :], ACT.Copy).then_inc(a_hi_ready, 1)

            def ffn_step(f, n, s, at=0, turn=0):
                for t in range(2):
                    silu(f, n, s, t, at)
                    split_hi(n + 3 * s + 2 + t, at, turn)
                    inner_hi(f, s, t, turn)
                split_hi(n + 3 * s + 4, at, turn)

            def ffn(f, first_unit):
                n = N_FFN[f]
                ffn_step(f, n, 0)
                load_ln_rows(NORM_OF_FFN[f])
                with act.Fori(0, LOOPS) as b:
                    for s in (1, 2):
                        ffn_step(f, n, s, at=6 * b, turn=b)
                    if first_unit is not None:
                        keep_unit(b + first_unit)
                ffn_step(f, n, STEPS - 2)
                s = STEPS - 1
                silu(f, n, s, 0)
                inner_hi(f, s, 0)
                if first_unit is not None:
                    keep_unit(first_unit + LOOPS)
                split_hi(n + 3 * s + 2)
                silu(f, n, s, 1)
                inner_hi(f, s, 1)
                nc.scalar.preload_act_table(ACT.Sqrt)
                keep_gate(NORM_OF_FFN[f])
                if f < 3:
                    split_hi(n + 3 * s + 3)
                    split_hi(n + 3 * s + 4)

            def keep_unit(u):
                act.wait_ge(unit_turned, u + 1)
                for k in range(KT):
                    src = misc[k // 4][:, (k % 4) * P:(k % 4 + 1) * P]
                    last = nc.scalar.activation(src, src, ACT.Copy,
                                                accum_out=modT[:, bass.ds(u, 1), k:k + 1].rearrange("p a k -> p (a k)"))
                last.then_inc(mod_ready, 1)

            def load_ln_rows(i):
                if i:
                    act.wait_ge(x_ready, 2 * i)
                act.dma_start(g_row[:, :], ln_g[i // 3, i % 3, :].partition_broadcast(P)).then_inc(ln_row_in, 16)
                act.dma_start(b_row[:, :], ln_b[i // 3, i % 3, :].partition_broadcast(P)).then_inc(ln_row_in, 16)

            def keep_gate(i):
                act.wait_ge(gate_spread, i + 1)
                nc.scalar.activation(gate[:, :], misc2, ACT.Copy, scale=GATE_W[i], bias=GATE_W[i])\
                  .then_inc(gate_ready, 1)

            def h_modulate(i, t):
                act.wait_ge(turned, 4 * i + 2 * t + 1)
                act.wait_ge(coef_ready, i + 1)
                for k in range(KT // 2):
                    last = nc.scalar.activation(h_fulls[t][:, k, :], tr_bank[t][0][:, k * P:(k + 1) * P], ACT.Identity,
                                                scale=coef[:, i, 0, k:k + 1], bias=coef[:, i, 1, k:k + 1])
                last.then_inc(h_act, 1)

            def h_hi(i, t):
                act.wait_ge(h_act, 2 * i + t + 1)
                nc.scalar.activation(hT_hi[:, 0:4, t * P:(t + 1) * P], h_fulls[t][:, 0:4, :], ACT.Copy)\
                  .then_inc(h_hi_ready, 1)
                act.wait_ge(h_dve, 2 * i + t + 1)
                nc.scalar.activation(hT_hi[:, 4:8, t * P:(t + 1) * P], h_fulls[t][:, 4:8, :], ACT.Copy)\
                  .then_inc(h_hi_ready, 1)

            def norm(i, h):
                for t in range(TT):
                    act.wait_ge(mean_ready, 2 * i + t + 1)
                    nc.scalar.activation(y_tok[t], z[:, t, :], ACT.Square, bias=nmean[:, t:t + 1],
                                         accum_out=sq[:, t:t + 1]).then_inc(sq_ready, 1)
                    act.wait_ge(sq_ready, 2 * i + t + 1)
                    nc.scalar.activation(sd[:, t:t + 1], sq[:, t:t + 1], ACT.Sqrt, scale=1.0 / D, bias=eps_t[:, 0:1])\
                      .then_inc(sd_ready, 1)
                    if h is not None:
                        h_modulate(h, t)
                        h_hi(h, t)

            def keep_yT(layer, h):
                act.wait_ge(pv_ready, HEADS * layer + h + 1)
                nc.scalar.activation(hT_hi[:, h, :], gu[h % 2][:, 0:SEQ], ACT.Copy).then_inc(yT_hi_ready, 1)

            act.dma_start(cond[:, :], c.rearrange("a (p k) -> p (a k)", k=8)).then_inc(c_in, 16)
            for r, w in enumerate((ln_g, ln_b)):
                act.dma_start(tmp[0:48, r * P:(r + 1) * P], w.rearrange("l s (k p) -> (l s k) p", p=P))\
                   .then_inc(lnT_in, 16)
            act.wait_ge(c_in, 16)
            nc.scalar.activation(cond[:, :], cond[:, :], ACT.Silu).then_inc(cond_ready, 1)
            act.wait_ge(lnT_turned, 1)
            nc.scalar.activation(lnT[:, :, :], misc[1][:, 0:96].rearrange("p (r n) -> p r n", r=2), ACT.Copy)\
              .then_inc(lnT_ready, 1)
            keep_unit(0)
            keep_unit(1)
            for t in range(TT):
                h_modulate(0, t)
                h_hi(0, t)
            split_hi(0)
            split_hi(1)
            ffn(0, unit(0, 2))
            norm(0, 1)
            n = N_QKV
            for i in range(8):
                split_hi(n + i + 2)
                if i == 1:
                    load_ln_rows(1)
                act.wait_ge(w_used, n + i + 1)
                if i == 0:
                    act.wait_ge(x_ready, 2)
                nc.scalar.activation((qT, kT)[i // 4][:, 2 * (i % 4):2 * (i % 4) + 2, :],
                                     gu[i % 2].rearrange("p (h t) -> p h t", h=2), ACT.Copy).then_inc(proj_kept, 1)
            nc.scalar.preload_act_table(ACT.Exp)

            def soft_exp(h):
                act.wait_ge(nmax_ready, h + 1)
                if h >= 2:
                    act.wait_ge(probT_ready, h - 1)
                nc.scalar.activation(prob[:, h % 2, 0:P], y[h % 2][:, 0:P], ACT.Exp, scale=SCALE,
                                     bias=nmx[:, h, 0:1], accum_out=rs[:, h, 0:1])
                nc.scalar.activation(prob[:, h % 2, P:384], y[h % 2][:, P:384], ACT.Exp, scale=SCALE,
                                     bias=nmx[:, h, 1:2], accum_out=rs[:, h, 1:2]).then_inc(exp_done, 1)

            def keep_probT(h):
                act.wait_ge(probT_ready, h + 1)
                nc.scalar.activation(qT[:, h, :], y[2 + h % 2][:, 0:SEQ], ACT.Copy)
                nc.scalar.activation(kT[:, h, 0:P], y[2 + h % 2][:, SEQ:384], ACT.Copy).then_inc(probT_kept, 1)

            for i in range(4):
                soft_exp(2 * i)
                split_hi(n + 8 + i + 2)
                soft_exp(2 * i + 1)
                act.wait_ge(w_used, n + 8 + i + 1)
                nc.scalar.activation(v_sb[:, :, 256 * i:256 * i + 256],
                                     gu[i % 2].rearrange("p (t n) -> p t n", t=2), ACT.Copy).then_inc(proj_kept, 1)
                if i == 0:
                    keep_unit(unit(0, 7))
                keep_probT(2 * i)
                keep_probT(2 * i + 1)
            nc.scalar.preload_act_table(ACT.Sqrt)
            for h in range(4):
                keep_yT(0, h)
            keep_gate(1)
            split_hi(N_WO[0] + 2)
            keep_yT(0, 4)
            keep_yT(0, 5)
            split_hi(N_WO[0] + 3)
            keep_yT(0, 6)
            keep_yT(0, 7)
            split_hi(N_WO[0] + 4)
            split_hi(N_WO[0] + 5)
            norm(1, 2)
            nc.scalar.preload_act_table(ACT.Silu)
            ffn(1, unit(0, 8))
            norm(2, 3)
            n = N_KV
            for i in range(8):
                split_hi(n + i + 2)
                if i == 7:
                    h_modulate(4, 0)
                    h_modulate(4, 1)
                act.wait_ge(w_used, n + i + 1)
                if i < 4:
                    nc.scalar.activation(kT[:, 2 * i:2 * i + 2, :], gu[i % 2].rearrange("p (h t) -> p h t", h=2),
                                         ACT.Copy).then_inc(proj_kept, 1)
                else:
                    nc.scalar.activation(v_sb[:, :, 256 * (i - 4):256 * (i - 4) + 256],
                                         gu[i % 2].rearrange("p (t n) -> p t n", t=2), ACT.Copy)\
                      .then_inc(proj_kept, 1)
            h_hi(4, 0)
            h_hi(4, 1)
            nc.scalar.preload_act_table(ACT.Silu)
            ffn(2, unit(1, 2))
            norm(3, 5)
            nc.scalar.preload_act_table_set("natural_log_exp_and_others")
            n = N_Q

            def stick_logs(h):
                act.wait_ge(z_ready, h + 1)
                if h >= 2:
                    act.wait_ge(pv_ready, HEADS + h - 1)
                nc.scalar.activation(prob[:, h % 2, :], y[h % 4][:, 0:384], ACT.Abs).then_inc(abs_done, 1)
                act.wait_ge(abs_done, h + 1)
                nc.scalar.activation(prob[:, h % 2, :], prob[:, h % 2, :], ACT.Exp, scale=-1.0).then_inc(expn_done, 1)
                act.wait_ge(expn_done, h + 1)
                nc.scalar.activation(prob[:, h % 2, :], prob[:, h % 2, :], ACT.Ln, bias=1.0).then_inc(ln1p_done, 1)

            def stick_weights(h):
                act.wait_ge(stick_ready, h + 1)
                nc.scalar.activation(prob[:, h % 2, :], y[h % 4][:, 0:384], ACT.Exp).then_inc(weight_ready, 1)

            for i in range(4):
                split_hi(n + i + 2)
                act.wait_ge(w_used, n + i + 1)
                if i == 0:
                    act.wait_ge(x_ready, 2 * 3 + 2)
                nc.scalar.activation(qT[:, 2 * i:2 * i + 2, :], gu[i % 2].rearrange("p (h t) -> p h t", h=2),
                                     ACT.Copy, scale=SCALE).then_inc(proj_kept, 1)
            load_ln_rows(4)
            split_hi(N_WO[1] + 2)
            keep_unit(unit(1, 7))
            keep_gate(4)
            for h in range(HEADS + 2):
                if h < HEADS:
                    stick_logs(h)
                if 1 <= h <= HEADS:
                    stick_weights(h - 1)
                if h >= 2:
                    keep_yT(1, h - 2)
            nc.scalar.preload_act_table(ACT.Sqrt)
            keep_unit(unit(1, 8))
            for j in range(1, 4):
                split_hi(N_WO[1] + j + 2)
            norm(4, 6)
            nc.scalar.preload_act_table(ACT.Silu)
            ffn(3, None)
            norm(5, None)

        @block.vector
        def _(dve):
            steps = [0]

            def own(instruction):
                steps[0] += 1
                instruction.then_inc(dve_step, 1)
                dve.wait_ge(dve_step, steps[0])

            def split_lo(n, at=0):
                dve.wait_ge(w_hi_ready, n + at + 1)
                nc.vector.tensor_tensor(w_lo[:, n % SPL, :], raw[:, n % RAW, :], w_hi[:, n % SPL, :].bitcast(F32),
                                        ALU.subtract).then_inc(w_lo_ready, 1)

            def accumulate(u, q):
                if isinstance(u, int) and 4 * u + q < STAGED:
                    src, landed = staged(4 * u + q)
                    dve.wait_ge(landed, 16)
                else:
                    src = ada[:, q % 2, :, :]
                    dve.wait_ge(ada_in[q % 2], 32 * u + (16 * (q // 2) + 16 - 8 * STAGED))
                if q == 0:
                    if not (isinstance(u, int) and u == 0):
                        dve.wait_ge(unit_turned, u)
                    dve.wait_ge(bias_in, 16 * u + 16)
                for r in range(2):
                    if not (isinstance(u, int) and u == 0 and q == 0 and r == 0):
                        dve.wait_ge(acc_steps, 8 * u + 2 * q + r)
                    nc.vector.scalar_tensor_tensor(out=acc[:, :], in0=src[:, r, :],
                                                   scalar=cond[:, 2 * q + r:2 * q + r + 1],
                                                   in1=bias0[:, :] if q == 0 and r == 0 else acc[:, :],
                                                   op0=ALU.mult, op1=ALU.add).then_inc(acc_steps, 1)

            def coefficients(i):
                shift, scale, norm_i = H_OF[i]
                dve.wait_ge(mod_ready, scale + 1)
                a, b = coef[:, i, 0, :], coef[:, i, 1, :]
                if norm_i is None:
                    nc.vector.tensor_copy(b, modT[:, shift, :])
                    nc.vector.tensor_scalar_add(a, modT[:, scale, :], 1.0).then_inc(coef_ready, 1)
                    return
                g_t = lnT[:, 0, norm_i * KT:(norm_i + 1) * KT]
                b_t = lnT[:, 1, norm_i * KT:(norm_i + 1) * KT]
                own(nc.vector.scalar_tensor_tensor(out=b, in0=modT[:, scale, :], scalar=1.0, in1=b_t,
                                                   op0=ALU.add, op1=ALU.mult))
                own(nc.vector.tensor_tensor(b, b, modT[:, shift, :], ALU.add))
                nc.vector.scalar_tensor_tensor(out=a, in0=modT[:, scale, :], scalar=1.0, in1=g_t,
                                               op0=ALU.add, op1=ALU.mult).then_inc(coef_ready, 1)

            def gate_diagonals(i):
                dve.wait_ge(mod_ready, GATE_OF[i] + 1)
                for k in range(KT):
                    last = nc.vector.tensor_scalar(h_full[:, k, :], ident, modT[:, GATE_OF[i], k:k + 1], None, ALU.mult)
                last.then_inc(diag_ready, 1)

            def inner(f, s, t, turn=0):
                dve.wait_ge(silu_ready, 2 * STEPS * f + 2 * s + t + 1 + 4 * turn)
                nc.vector.tensor_tensor(a_full[:, t, :], gu[t][:, SEQ:2 * SEQ], silu_t[:, t, :], ALU.mult)\
                  .then_inc(a_ready, 1)

            def inner_lo(f, s, t, turn=0):
                dve.wait_ge(a_hi_ready, 2 * STEPS * f + 2 * s + t + 1 + 4 * turn)
                nc.vector.tensor_tensor(a_lo[:, s % 2, t, :], a_full[:, t, :], a_hi[:, s % 2, t, :].bitcast(F32),
                                        ALU.subtract).then_inc(a_lo_ready, 1)

            def ffn_step(f, n, s, at=0, turn=0, u=None, parts=((), (), ())):
                for t in range(2):
                    inner(f, s, t, turn)
                    for q in parts[t]:
                        accumulate(u, q)
                    split_lo(n + 3 * s + 2 + t, at)
                    inner_lo(f, s, t, turn)
                for q in parts[2]:
                    accumulate(u, q)
                split_lo(n + 3 * s + 4, at)

            def ffn(f, first_unit, before_gate):
                n = N_FFN[f]
                ffn_step(f, n, 0)
                with dve.Fori(0, LOOPS) as b:
                    if first_unit is None:
                        for s in (1, 2):
                            ffn_step(f, n, s, at=6 * b, turn=b)
                    else:
                        u = b + first_unit
                        ffn_step(f, n, 1, at=6 * b, turn=b, u=u, parts=((0,), (1,), ()))
                        ffn_step(f, n, 2, at=6 * b, turn=b, u=u, parts=((2,), (3,), ()))
                if first_unit is None:
                    ffn_step(f, n, STEPS - 2)
                else:
                    ffn_step(f, n, STEPS - 2, u=first_unit + LOOPS, parts=((0, 1), (2,), (3,)))
                s = STEPS - 1
                inner(f, s, 0)
                inner_lo(f, s, 0)
                for i in before_gate:
                    coefficients(i)
                gate_diagonals(NORM_OF_FFN[f])
                split_lo(n + 3 * s + 2)
                inner(f, s, 1)
                inner_lo(f, s, 1)
                if f < 3:
                    split_lo(n + 3 * s + 3)
                    split_lo(n + 3 * s + 4)

            def h_modulate(i, t):
                dve.wait_ge(turned, 4 * i + 2 * t + 2)
                dve.wait_ge(coef_ready, i + 1)
                for k in range(KT // 2, KT):
                    last = nc.vector.tensor_scalar(h_fulls[t][:, k, :], tr_bank[t][1][:, (k - 4) * P:(k - 3) * P],
                                                   coef[:, i, 0, k:k + 1], coef[:, i, 1, k:k + 1], ALU.mult, ALU.add)
                last.then_inc(h_dve, 1)

            def h_lo(i, t):
                for half in range(2):
                    dve.wait_ge(h_hi_ready, 4 * i + 2 * t + half + 1)
                    nc.vector.tensor_tensor(hT_lo[:, 4 * half:4 * half + 4, t * P:(t + 1) * P],
                                            h_fulls[t][:, 4 * half:4 * half + 4, :],
                                            hT_hi[:, 4 * half:4 * half + 4, t * P:(t + 1) * P].bitcast(F32),
                                            ALU.subtract).then_inc(h_lo_ready, 1)

            def residual(i, t):
                if t == 0:
                    dve.wait_ge(y_ready, i + 1)
                else:
                    dve.wait_ge(w_used, LAST_CHUNK[i] + 1)
                dve.wait_ge(gate_ready, i + 1)
                own(nc.vector.tensor_tensor(z[:, t, :], y_tok[t], gate[:, :], ALU.mult))
                own(nc.vector.scalar_tensor_tensor(out=z[:, t, :], in0=x_sb[:, t, :], scalar=ALPHA, in1=z[:, t, :],
                                                   op0=ALU.mult, op1=ALU.add, accum_out=total[:, t:t + 1]))
                nc.vector.tensor_scalar(nmean[:, t:t + 1], total[:, t:t + 1], -1.0 / D, None, ALU.mult)\
                  .then_inc(mean_ready, 1)

            def normalise(i, t):
                dve.wait_ge(sd_ready, 2 * i + t + 1)
                own(nc.vector.reciprocal(rstd[:, t:t + 1], sd[:, t:t + 1]))
                nc.vector.tensor_scalar(z[:, t, :], z[:, t, :], nmean[:, t:t + 1], rstd[:, t:t + 1],
                                        ALU.add, ALU.mult).then_inc(xn_ready, 1)

            def new_x(i, t):
                dve.wait_ge(ln_row_in, 32 * (i + 1))
                dve.wait_ge(xn_ready, 2 * i + t + 1)
                own(nc.vector.tensor_tensor(x_sb[:, t, :], z[:, t, :], g_row[:, :], ALU.mult))
                nc.vector.tensor_tensor(x_sb[:, t, :], x_sb[:, t, :], b_row[:, :], ALU.add).then_inc(x_ready, 1)

            def norm(i, h):
                for t in range(TT):
                    residual(i, t)
                    normalise(i, t)
                    if h is not None:
                        h_modulate(h, t)
                        h_lo(h, t)
                    else:
                        new_x(i, t)
                if h is not None:
                    for t in range(TT):
                        new_x(i, t)

            def keep_yT(layer, h):
                dve.wait_ge(yT_hi_ready, HEADS * layer + h + 1)
                nc.vector.tensor_tensor(hT_lo[:, h, :], gu[h % 2][:, 0:SEQ], hT_hi[:, h, :].bitcast(F32),
                                        ALU.subtract).then_inc(yT_lo_ready, 1)

            nc.vector.memset(eps_t[:, :], EPS)
            nc.vector.memset(all_ones[:, :], 1.0)
            nc.vector.memset(neg_ones[:, :], -1.0)
            nc.vector.memset(zeros[:, :], 0.0)
            nc.vector.memset(bias0[:, :], 0.0).then_inc(set_up, 1)
            dve.wait_ge(cond_ready, 1)
            for u in range(2):
                for q in range(4):
                    accumulate(u, q)
            coefficients(0)
            for t in range(TT):
                h_modulate(0, t)
                h_lo(0, t)
            split_lo(0)
            split_lo(1)
            ffn(0, unit(0, 2), (1,))
            norm(0, 1)
            n = N_QKV

            def rope(i):
                side = (qT, kT)[i // 4][0:ROT, 2 * (i % 4):2 * (i % 4) + 2, :]
                two = [ROT, 2, SEQ]
                dve.wait_ge(rot_ready, i + 1)
                if i:
                    dve.wait_ge(rope_done, i)
                own(nc.vector.tensor_tensor(rope_t.rearrange("p (h t) -> p h t", h=2),
                                            misc[i % 2][0:ROT, :].rearrange("p (h t) -> p h t", h=2),
                                            sin_t.unsqueeze(1).to_broadcast(two), ALU.mult))
                own(nc.vector.tensor_tensor(side, side, cos_t.unsqueeze(1).to_broadcast(two), ALU.mult))
                nc.vector.tensor_tensor(side, side, rope_t.rearrange("p (h t) -> p h t", h=2), ALU.add)\
                  .then_inc(rope_done, 1)

            for i in range(8):
                split_lo(n + i + 2)
                if i >= 1:
                    rope(i - 1)
                if i < 4:
                    accumulate(unit(0, 7), i)
            rope(7)

            def soft_max(h):
                dve.wait_ge(score_ready, h + 1)
                nc.vector.reduce_max(mx[:, h, 0:1], y[h % 2][:, 0:P], AX.X)
                own(nc.vector.reduce_max(mx[:, h, 1:2], y[h % 2][:, P:384], AX.X))
                nc.vector.tensor_scalar(nmx[:, h, :], mx[:, h, :], -SCALE, None, ALU.mult).then_inc(nmax_ready, 1)

            def soft_scale(h):
                dve.wait_ge(exp_done, h + 1)
                own(nc.vector.reciprocal(rinv[:, h, :], rs[:, h, :]))
                nc.vector.tensor_scalar(prob[:, h % 2, 0:P], prob[:, h % 2, 0:P], rinv[:, h, 0:1], None, ALU.mult)
                nc.vector.tensor_scalar(prob[:, h % 2, P:384], prob[:, h % 2, P:384], rinv[:, h, 1:2], None,
                                        ALU.mult).then_inc(prob_ready, 1)

            for i in range(4):
                soft_max(2 * i)
                soft_max(2 * i + 1)
                soft_scale(2 * i)
                split_lo(n + 8 + i + 2)
                soft_scale(2 * i + 1)
            coefficients(2)
            gate_diagonals(1)
            for h in range(4):
                keep_yT(0, h)
            split_lo(N_WO[0] + 2)
            keep_yT(0, 4)
            keep_yT(0, 5)
            split_lo(N_WO[0] + 3)
            keep_yT(0, 6)
            keep_yT(0, 7)
            split_lo(N_WO[0] + 4)
            split_lo(N_WO[0] + 5)
            norm(1, 2)
            ffn(1, unit(0, 8), (3,))
            norm(2, 3)
            for i in range(8):
                split_lo(N_KV + i + 2)
                if i == 0:
                    coefficients(4)
            for t in range(TT):
                h_modulate(4, t)
            for t in range(TT):
                h_lo(4, t)
            ffn(2, unit(1, 2), (5,))
            norm(3, 5)
            for i in range(4):
                split_lo(N_Q + i + 2)
                accumulate(unit(1, 7), i)
            coefficients(6)
            gate_diagonals(4)
            split_lo(N_WO[1] + 2)

            def stick_sums(h):
                dve.wait_ge(ln1p_done, h + 1)
                own(nc.vector.scalar_tensor_tensor(out=sp_t[:, h % 2, :], in0=y[h % 4][:, 0:384], scalar=0.0,
                                                   in1=prob[:, h % 2, :], op0=ALU.max, op1=ALU.add))
                nc.vector.tensor_tensor(sp_t[:, h % 2, 0:P], sp_t[:, h % 2, 0:P], keep, ALU.mult)
                nc.vector.tensor_tensor(sp_t[:, h % 2, SEQ:384], sp_t[:, h % 2, SEQ:384], keep, ALU.mult)\
                  .then_inc(keepsum_ready, 1)

            for h in range(HEADS + 2):
                if h < HEADS:
                    stick_sums(h)
                    if h % 2 == 1:
                        accumulate(unit(1, 8), h // 2)
                if h >= 2:
                    keep_yT(1, h - 2)
            for j in range(1, 4):
                split_lo(N_WO[1] + j + 2)
            norm(4, 6)
            ffn(3, None, ())
            norm(5, None)

        @block.tensor
        def _(pe):
            def three(dst, stat, mov, start, stop):
                (s_hi, s_lo), (m_hi, m_lo) = stat, mov
                nc.tensor.matmul(dst, s_hi, m_hi, start=start, stop=False)
                nc.tensor.matmul(dst, s_hi, m_lo, start=False, stop=False)
                return nc.tensor.matmul(dst, s_lo, m_hi, start=False, stop=stop)

            def w_cols(n, k, j, inner):
                at, width = (j * 1024 + k * P if inner else k * 256 + j * P), P
                return w_hi[:, n % SPL, at:at + width], w_lo[:, n % SPL, at:at + width]

            def w_wide(n, k):
                at = k * 256
                return w_hi[:, n % SPL, at:at + 256], w_lo[:, n % SPL, at:at + 256]

            def w_rows(n, j, half):
                at = j * 1024 + half * 512
                return w_hi[:, n % SPL, at:at + 512], w_lo[:, n % SPL, at:at + 512]

            def h_all(k):
                return hT_hi[:, k, :], hT_lo[:, k, :]

            def h_tok(k, t):
                return hT_hi[:, k, t * P:(t + 1) * P], hT_lo[:, k, t * P:(t + 1) * P]

            def turn_tile(src, t):
                for k in range(KT):
                    last = nc.tensor.transpose(tr_bank[t][k // 4][:, (k % 4) * P:(k % 4 + 1) * P],
                                               src[:, t, k * P:(k + 1) * P], ident)
                    if k % 4 == 3:
                        last.then_inc(turned, 1)

            def turn_unit(u):
                pe.wait_ge(acc_steps, 8 * u + 8)
                for k in range(KT):
                    last = nc.tensor.transpose(misc[k // 4][:, (k % 4) * P:(k % 4 + 1) * P],
                                               acc[:, k * P:(k + 1) * P], ident)
                last.then_inc(unit_turned, 1)

            def spread_gate(i):
                pe.wait_ge(diag_ready, i + 1)
                for k in range(KT):
                    last = nc.tensor.matmul(misc[k // 4][:, (k % 4) * P:(k % 4 + 1) * P], all_ones[:, :],
                                            h_full[:, k, :], start=True, stop=True)
                last.then_inc(gate_spread, 1)

            def columns_out(n, dst, inner=False, at=0):
                pe.wait_ge(w_lo_ready, n + at + 1)
                for j in range(2):
                    for k in range(KT):
                        last = three(dst[:, j * SEQ:(j + 1) * SEQ], w_cols(n, k, j, inner), h_all(k),
                                     k == 0, k == KT - 1)
                last.then_inc(w_used, 1)

            def tokens_out(n, dst):
                pe.wait_ge(w_lo_ready, n + 1)
                for t in range(TT):
                    for k in range(KT):
                        last = three(dst[:, t * 256:(t + 1) * 256], h_tok(k, t), w_wide(n, k),
                                     k == 0, k == KT - 1)
                last.then_inc(w_used, 1)

            def first_pair(n, h, src, ready, inner=False):
                if src is not None:
                    for t in range(TT):
                        pe.wait_ge(*ready(t))
                        turn_tile(src, t)
                pe.wait_ge(h_lo_ready, 4 * h + 4)
                for c in range(2):
                    columns_out(n + c, gu[c], inner)

            def add_rows(n, operand, t, first=False, last=False, at=0):
                for j in range(2):
                    hi, lo = operand(j, t)
                    for half in range(2):
                        m = w_rows(n, j, half)
                        dst = y[2 * t + half]
                        nc.tensor.matmul(dst, hi, m[0], start=first and j == 0, stop=False)
                        nc.tensor.matmul(dst, hi, m[1], start=False, stop=False)
                        end = nc.tensor.matmul(dst, lo, m[0], start=False, stop=last and j == 1)
                return end

            def last_pair(n, operands, waits):
                for t in range(TT):
                    for c in range(2):
                        if t == 0:
                            pe.wait_ge(w_lo_ready, n + c + 1)
                            pe.wait_ge(*waits[c])
                        end = add_rows(n + c, operands[c], t, last=c == 1)
                        if t == 1:
                            end.then_inc(w_used, 1)
                    if t == 0:
                        end.then_inc(y_ready, 1)

            def in_tile(f, n, s, t, at=0, turn=0):
                pe.wait_ge(a_ready, 2 * STEPS * f + 2 * s + t - 1 + 4 * turn)
                columns_out(n + 3 * s - 1 + t, gu[t], inner=True, at=at)

            def inner(s):
                return lambda j, t: (a_hi[:, s % 2, j, t * P:(t + 1) * P], a_lo[:, s % 2, j, t * P:(t + 1) * P])

            def inner_done(f, s, turn=0):
                return a_lo_ready, 2 * STEPS * f + 2 * s + 2 + 4 * turn

            def ffn_out(f, n, s, at=0, turn=0):
                pe.wait_ge(*inner_done(f, s, turn))
                pe.wait_ge(w_lo_ready, n + 3 * s + 4 + at + 1)
                add_rows(n + 3 * s + 4, inner(s), 0)
                add_rows(n + 3 * s + 4, inner(s), 1).then_inc(w_used, 1)

            def ffn(f, first_unit, src, ready):
                n = N_FFN[f]
                first_pair(n, H_OF_FFN[f], src, ready, inner=True)
                for i in range(4):
                    nc.tensor.matmul(y[i], zeros[:, 0:P], zeros[:, :], start=True, stop=False)
                with pe.Fori(0, LOOPS) as b:
                    for s in (1, 2):
                        for t in range(2):
                            in_tile(f, n, s, t, at=6 * b, turn=b)
                        ffn_out(f, n, s - 1, at=6 * b, turn=b)
                    if first_unit is not None:
                        turn_unit(b + first_unit)
                for t in range(2):
                    in_tile(f, n, STEPS - 2, t)
                ffn_out(f, n, STEPS - 3)
                in_tile(f, n, STEPS - 1, 0)
                if first_unit is not None:
                    turn_unit(first_unit + LOOPS)
                in_tile(f, n, STEPS - 1, 1)
                if first_unit is not None:
                    pe.wait_ge(mod_ready, first_unit + LOOPS + 1)
                spread_gate(NORM_OF_FFN[f])
                last_pair(n + FFN_CHUNKS - 2, (inner(STEPS - 2), inner(STEPS - 1)),
                          (inner_done(f, STEPS - 2), inner_done(f, STEPS - 1)))

            def normed(i):
                return lambda t: (xn_ready, 2 * i + t + 1)

            def weigh_values(layer, h, first, second):
                if h >= 2:
                    pe.wait_ge(yT_lo_ready, HEADS * layer + h - 1)
                nc.tensor.matmul(gu[h % 2][:, 0:SEQ], v_sb[:, 0, h * DH:(h + 1) * DH], first, start=True, stop=False)
                nc.tensor.matmul(gu[h % 2][:, P:SEQ], v_sb[:, 1, h * DH:(h + 1) * DH], second, start=False, stop=True)\
                  .then_inc(pv_ready, 1)

            def heads_pair(j):
                return lambda jj, t: h_tok(2 * j + jj, t)

            def output_rows(layer, j):
                pe.wait_ge(yT_lo_ready, HEADS * layer + 2 * j + 2)
                pe.wait_ge(w_lo_ready, N_WO[layer] + j + 1)
                add_rows(N_WO[layer] + j, heads_pair(j), 0, first=j == 0)
                add_rows(N_WO[layer] + j, heads_pair(j), 1, first=j == 0).then_inc(w_used, 1)

            def output_end(layer):
                last_pair(N_WO[layer] + 2, (heads_pair(2), heads_pair(3)),
                          ((yT_lo_ready, HEADS * layer + 6), (yT_lo_ready, HEADS * layer + 8)))

            pe.wait_ge(set_up, 1)
            pe.wait_ge(cst_in, 16)
            pe.wait_ge(lnT_in, 32)
            for r in range(2):
                last = nc.tensor.transpose(misc[1][:, 48 * r:48 * r + 48], tmp[0:48, r * P:(r + 1) * P],
                                           ident[0:48, 0:48])
            last.then_inc(lnT_turned, 1)
            pe.wait_ge(lnT_ready, 1)
            turn_unit(0)
            pe.wait_ge(mod_ready, 1)
            turn_unit(1)
            pe.wait_ge(mod_ready, 2)
            pe.wait_ge(x_in, 16 * TT)
            turn_tile(x_sb, 0)
            turn_tile(x_sb, 1)
            ffn(0, unit(0, 2), None, None)

            def rotate(i):
                pe.wait_ge(proj_kept, i + 1)
                if i >= 2:
                    pe.wait_ge(rope_done, i - 1)
                nc.tensor.matmul(misc[i % 2], rot_m,
                                 (qT, kT)[i // 4][0:ROT, 2 * (i % 4):2 * (i % 4) + 2, :].rearrange("p h t -> p (h t)"),
                                 start=True, stop=True).then_inc(rot_ready, 1)

            first_pair(N_QKV, 1, z, normed(0))
            rotate(0)
            for i in range(2, 8):
                pe.wait_ge(proj_kept, i - 1)
                columns_out(N_QKV + i, gu[i % 2])
                rotate(i - 1)
            rotate(7)

            def scores(h):
                if h >= 2:
                    pe.wait_ge(exp_done, h - 1)
                s = y[h % 2]
                nc.tensor.matmul(s[:, 0:P], qT[:, h, 0:P], kT[:, h, 0:P], start=True, stop=False)
                nc.tensor.matmul(s[:, 0:P], ident, causal, start=False, stop=True)
                nc.tensor.matmul(s[:, P:384], qT[:, h, P:SEQ], kT[:, h, :], start=True, stop=False)
                nc.tensor.matmul(s[:, SEQ:384], ident, causal, start=False, stop=True).then_inc(score_ready, 1)

            def turn_probs(h):
                pe.wait_ge(prob_ready, h + 1)
                if h >= 2:
                    pe.wait_ge(probT_kept, h - 1)
                for b in range(3):
                    last = nc.tensor.transpose(y[2 + h % 2][:, b * P:(b + 1) * P], prob[:, h % 2, b * P:(b + 1) * P],
                                               ident)
                last.then_inc(probT_ready, 1)

            pe.wait_ge(rope_done, 8)
            for i in range(4):
                scores(2 * i)
                scores(2 * i + 1)
                pe.wait_ge(proj_kept, 8 + i - 1)
                tokens_out(N_QKV + 8 + i, gu[i % 2])
                if i == 0:
                    turn_unit(unit(0, 7))
                turn_probs(2 * i)
                turn_probs(2 * i + 1)
            pe.wait_ge(proj_kept, 12)
            pe.wait_ge(probT_kept, HEADS)
            for h in range(4):
                weigh_values(0, h, qT[:, h, :], kT[:, h, 0:P])
            spread_gate(1)
            for j in range(2):
                output_rows(0, j)
                for h in (2 * j + 4, 2 * j + 5):
                    weigh_values(0, h, qT[:, h, :], kT[:, h, 0:P])
            output_end(0)
            ffn(1, unit(0, 8), z, normed(1))
            first_pair(N_KV, 3, z, normed(2))
            for i in range(2, 8):
                if i == 7:
                    pe.wait_ge(x_ready, 2 * 2 + 2)
                    turn_tile(x_sb, 0)
                    turn_tile(x_sb, 1)
                pe.wait_ge(proj_kept, 12 + i - 1)
                if i < 4:
                    columns_out(N_KV + i, gu[i % 2])
                else:
                    tokens_out(N_KV + i, gu[i % 2])
            pe.wait_ge(proj_kept, 20)
            ffn(2, unit(1, 2), None, None)
            first_pair(N_Q, 5, z, normed(3))
            for i in range(2, 4):
                pe.wait_ge(proj_kept, 20 + i - 1)
                columns_out(N_Q + i, gu[i % 2])
            turn_unit(unit(1, 7))
            pe.wait_ge(mod_ready, unit(1, 7) + 1)
            spread_gate(4)
            pe.wait_ge(proj_kept, 24)

            def stick_scores(h):
                s = y[h % 4]
                nc.tensor.matmul(s[:, 0:SEQ], kT[:, h, 0:P], qT[:, h, :], start=True, stop=True)
                nc.tensor.matmul(s[:, SEQ:384], kT[:, h, P:SEQ], qT[:, h, P:SEQ], start=False, stop=True,
                                 skip_group_check=True).then_inc(z_ready, 1)

            def stick_log_weights(h):
                pe.wait_ge(keepsum_ready, h + 1)
                s, first, second = y[h % 4], sp_t[:, h % 2, 0:SEQ], sp_t[:, h % 2, SEQ:384]
                for dst, stat, mov in ((s[:, 0:SEQ], tri, first), (s[:, P:SEQ], neg_ones[:, :], second),
                                       (s[:, SEQ:384], tri, second), (s[:, 0:P], ident, strict),
                                       (s[:, SEQ:384], ident, strict)):
                    last = nc.tensor.matmul(dst, stat, mov, start=False, stop=True, skip_group_check=True)
                last.then_inc(stick_ready, 1)

            for h in range(HEADS + 2):
                if h < HEADS:
                    stick_scores(h)
                if h >= 2:
                    pe.wait_ge(weight_ready, h - 1)
                    weigh_values(1, h - 2, prob[:, h % 2, 0:SEQ], prob[:, h % 2, SEQ:384])
                if 1 <= h <= HEADS:
                    stick_log_weights(h - 1)
            turn_unit(unit(1, 8))
            for j in range(2):
                output_rows(1, j)
            output_end(1)
            ffn(3, None, z, normed(4))


_INS = ["x", "c", "w_ada", "b_ada", "ln_g", "ln_b", "w_ffn_in", "w_ffn_out", "w_qkv_a", "w_q_b",
        "w_kv_ada", "b_kv_ada", "w_kv_b", "w_o"]


def shape_constants():
    row, col = np.arange(P)[:, None], np.arange(P)[None, :]
    a = np.zeros((P, C_ALL), np.float32)
    a[:, C_ID:C_ID + P] = row == col
    a[:, C_TRI:C_TRI + P] = np.where(row >= col, -1.0, 0.0)
    a[:, C_CAUSAL:C_CAUSAL + P] = np.where(col > row, -1e30, 0.0)
    a[:, C_STRICT:C_STRICT + P] = np.where(row >= col, -1e30, 0.0)
    a[:, C_KEEP:C_KEEP + P] = row < col
    half = ROT // 2
    freq = np.power(np.float32(500000.0), -np.arange(half, dtype=np.float32) * np.float32(2.0) / np.float32(ROT))
    angle = np.arange(SEQ, dtype=np.float32)[None, :] * freq.astype(np.float32)[:, None]
    for i in range(2):
        a[i * half:(i + 1) * half, C_COS:C_COS + SEQ] = np.cos(angle)
        a[i * half:(i + 1) * half, C_SIN:C_SIN + SEQ] = np.sin(angle)
    for i in range(half):
        a[i + half, C_ROT + i] = -1.0
        a[i, C_ROT + i + half] = 1.0
    return a


def kernel(**inputs):
    import concourse.bacc as bacc
    from concourse.bass_utils import run_bass_kernel_spmd

    nc = bacc.Bacc("TRN2", target_bir_lowering=False, num_devices=1)
    arrays, args = {}, []
    for name in _INS:
        a = np.ascontiguousarray(inputs[name])
        arrays["in_" + name] = a
        args.append(nc.dram_tensor("in_" + name, a.shape, mybir.dt.from_np(a.dtype), kind="ExternalInput").ap())
    arrays["in_consts"] = shape_constants()
    args.append(nc.dram_tensor("in_consts", (P, C_ALL), F32, kind="ExternalInput").ap())
    args.append(nc.dram_tensor("out", (1, SEQ, D), F32, kind="ExternalOutput").ap())
    build(nc, *args)
    r = run_bass_kernel_spmd(nc, [arrays], core_ids=[0])
    return r.results[0]["out"]
```

```python
from contextlib import ExitStack

import numpy as np

import concourse.bass as bass
from concourse import mybir

F32 = mybir.dt.float32
F32R = mybir.dt.float32r
BF16 = mybir.dt.bfloat16
ACT = mybir.ActivationFunctionType
ALU = mybir.AluOpType
AX = mybir.AxisListType

P = 128
D = 1024
SEQ = 256
KT = D // P
TT = SEQ // P
HEADS = 8
DH = D // HEADS
ROT = DH // 4
DFF = 2816
STEPS = DFF // 256
LOOPS = (STEPS - 3) // 2
DEPTH = 2
ALPHA = (2.0 * DEPTH) ** 0.25
EPS = 1e-5
SCALE = DH ** -0.5
CH = 2048
RAW = 6
STAGED = 8
SPL = 3
MODS = 9

FFN_CHUNKS = 3 * STEPS
N_FFN = [0] * 4
N_FFN[0] = 0
N_QKV = N_FFN[0] + FFN_CHUNKS
N_WO = [N_QKV + 12, 0]
N_FFN[1] = N_WO[0] + 4
N_KV = N_FFN[1] + FFN_CHUNKS
N_FFN[2] = N_KV + 8
N_Q = N_FFN[2] + FFN_CHUNKS
N_WO[1] = N_Q + 4
N_FFN[3] = N_WO[1] + 4
N_ALL = N_FFN[3] + FFN_CHUNKS

KV = 2
ORDER = [(0, 0), (0, 1), (0, 3), (0, 4), (0, 6), (0, 7), (0, 2), (0, 5),
         (KV, 0), (KV, 1), (1, 0), (1, 1), (0, 8),
         (1, 3), (1, 4), (1, 6), (1, 7), (1, 2), (1, 5), (1, 8)]
UNITS = len(ORDER)
BIAS_AT = [{0: 0, KV: MODS, 1: MODS + 2}[layer] + j for layer, j in ORDER]


def unit(layer, j):
    return ORDER.index((layer, j))


H_OF = [(unit(0, 0), unit(0, 1), None),
        (unit(0, 3), unit(0, 4), 0),
        (unit(0, 6), unit(0, 7), 1),
        (unit(KV, 0), unit(KV, 1), 2),
        (unit(1, 0), unit(1, 1), None),
        (unit(1, 3), unit(1, 4), 3),
        (unit(1, 6), unit(1, 7), 4)]
GATE_OF = [unit(0, 2), unit(0, 5), unit(0, 8), unit(1, 2), unit(1, 5), unit(1, 8)]


def kept(u):
    return sum(v not in GATE_OF for v in range(u + 1))


FIRST_UNIT = [unit(0, 3), unit(KV, 0), unit(1, 3), None]
START_PRODUCTS = (24, 24)
WAIT_PRODUCTS = (13, 6)
GATE_W = [0.5, 1.0, 0.5, 0.5, 1.0, 0.5]
C_ID, C_TRI, C_CAUSAL, C_STRICT, C_KEEP, C_COS, C_SIN, C_ROT = (
    0, 128, 256, 384, 512, 640, 896, 1152)
C_ALL = 1280
NORM_OF_FFN = [0, 2, 3, 5]
LAST_CHUNK = [N_FFN[0] + FFN_CHUNKS - 1, N_WO[0] + 3, N_FFN[1] + FFN_CHUNKS - 1,
              N_FFN[2] + FFN_CHUNKS - 1, N_WO[1] + 3, N_FFN[3] + FFN_CHUNKS - 1]
H_OF_FFN = [0, 2, 4, 6]


def build(nc, x, c, w_ada, b_ada, ln_g, ln_b, w_ffn_in, w_ffn_out, w_qkv_a, w_q_b,
          w_kv_ada, b_kv_ada, w_kv_b, w_o, consts, out):
    ctx = ExitStack()
    with ctx:
        def sb(name, shape, dt=F32):
            return ctx.enter_context(nc.sbuf_tensor(name, shape, dt))

        def sem(name):
            return ctx.enter_context(nc.semaphore(name))

        raw = sb("raw", [P, RAW, CH])
        w_hi = sb("w_hi", [P, SPL, CH], F32R)
        w_lo = sb("w_lo", [P, SPL, CH], F32R)
        ada = sb("ada", [P, 2, 2, 1024])
        acc = sb("acc", [P, 1024])
        bias0 = sb("bias0", [P, 1024])
        x_sb = sb("x_sb", [P, TT, D])
        hT_hi = sb("hT_hi", [P, KT, SEQ], F32R)
        hT_lo = sb("hT_lo", [P, KT, SEQ], F32R)
        a_hi = sb("a_hi", [P, 2, 2, SEQ], F32R)
        a_lo = sb("a_lo", [P, 2, 2, SEQ], F32R)
        tmp = sb("tmp", [P, 1536])
        h_full = sb("h_full", [P, KT, P])
        gate = sb("gate", [P, D])
        g_row = sb("g_row", [P, D])
        b_row = sb("b_row", [P, D])
        qT = sb("qT", [P, HEADS, SEQ])
        kT = sb("kT", [P, HEADS, SEQ])
        v_sb = sb("v_sb", [P, TT, D])
        cst = sb("cst", [P, C_ALL])
        modT = sb("modT", [P, UNITS, KT])
        coef = sb("coef", [P, len(H_OF), 2, KT])
        rowsT = sb("rowsT", [P, 256])
        cond = sb("cond", [P, 8])
        total = sb("total", [P, TT + 1])
        nmean = sb("nmean", [P, TT])
        sq = sb("sq", [P, TT])
        sd = sb("sd", [P, TT])
        rstd = sb("rstd", [P, TT])
        neg_ones = sb("neg_ones", [P, P])
        zeros = sb("zeros", [P, 512], BF16)
        masks = sb("masks", [P, 3, P], BF16)
        eps_t = sb("eps_t", [P, 1])
        mx = sb("mx", [P, HEADS, 2])
        nmx = sb("nmx", [P, HEADS, 2])
        rs = sb("rs", [P, HEADS, 2])
        rinv = sb("rinv", [P, HEADS, 2])

        lnT = rowsT[:, 0:96].rearrange("p (r n) -> p r n", r=2)
        biasT = rowsT[:, 96:256].rearrange("p (u k) -> p u k", k=KT)
        acc0 = tmp[:, 512:1536]
        ident = cst[:, C_ID:C_ID + P]
        tri = cst[:, C_TRI:C_TRI + P]
        causal = cst[:, C_CAUSAL:C_CAUSAL + P]
        strict = cst[:, C_STRICT:C_STRICT + P]
        keep = cst[:, C_KEEP:C_KEEP + P]
        ident_b, causal_b, strict_b = (masks[:, i, :] for i in range(3))
        cos_t = cst[0:ROT, C_COS:C_COS + SEQ]
        sin_t = cst[0:ROT, C_SIN:C_SIN + SEQ]
        rot_m = cst[0:ROT, C_ROT:C_ROT + P]
        silu_t = tmp[:, 0:512].rearrange("p (j t) -> p j t", j=2)
        a_full = tmp[:, 512:1024].rearrange("p (j t) -> p j t", j=2)
        prob = tmp[:, 0:768].rearrange("p (j t) -> p j t", j=2)
        stick = tmp[:, :].rearrange("p (j t) -> p j t", j=4)
        sp_t = h_full[:, 0:6, :].rearrange("p (j k) t -> p j (k t)", j=2)
        rope_t = tmp[0:ROT, 1024:1536]
        z = qT[:, :, :].rearrange("p (t h) s -> p t (h s)", t=TT)
        h_fulls = [h_full[:, :, :], tmp[:, 0:1024].rearrange("p (k t) -> p k t", k=KT)]

        psum = ctx.enter_context(nc.psum_tensor("psum", [P, 8, 512], F32))
        gu = [psum[:, 0, :], psum[:, 1, :]]
        misc = [psum[:, 2, :], psum[:, 3, :]]
        misc2 = psum[:, 2:4, :].rearrange("p b n -> p (b n)")
        y = [psum[:, 4 + i, :] for i in range(4)]
        y_tok = [psum[:, 4 + 2 * t:6 + 2 * t, :].rearrange("p b n -> p (b n)") for t in range(TT)]
        tr_bank = [misc, y[0:2]]
        start_bank = [y[2:4], y[0:2]]

        raw_in = [sem(f"raw_in{i}") for i in range(RAW)]
        w_hi_ready = sem("w_hi_ready")
        w_lo_ready = sem("w_lo_ready")
        w_used = sem("w_used")
        ada_in = [sem(f"ada_in{i}") for i in range(2)]
        staged_in = [sem(f"staged_in{i}") for i in range(3)]
        bias_in = sem("bias_in")
        acc_steps = sem("acc_steps")
        unit_out = sem("unit_out")
        mod_ready = sem("mod_ready")
        second_half_kept = sem("second_half_kept")
        masks_ready = sem("masks_ready")
        cst_in = sem("cst_in")
        x_in = sem("x_in")
        c_in = sem("c_in")
        rows_in = sem("rows_in")
        set_up = sem("set_up")
        cond_ready = sem("cond_ready")
        rows_turned = sem("rows_turned")
        rows_ready = sem("rows_ready")
        ln_row_in = sem("ln_row_in")
        turned = sem("turned")
        h_act = sem("h_act")
        h_dve = sem("h_dve")
        h_hi_ready = sem("h_hi_ready")
        h_lo_ready = sem("h_lo_ready")
        coef_ready = sem("coef_ready")
        silu_ready = sem("silu_ready")
        a_ready = sem("a_ready")
        a_hi_ready = sem("a_hi_ready")
        a_lo_ready = sem("a_lo_ready")
        gate_ready = sem("gate_ready")
        kv_tile_done = sem("kv_tile_done")
        y_ready = sem("y_ready")
        dve_step = sem("dve_step")
        mean_ready = sem("mean_ready")
        sq_ready = sem("sq_ready")
        sd_ready = sem("sd_ready")
        xn_ready = sem("xn_ready")
        centre_done = sem("centre_done")
        x_scaled_done = sem("x_scaled_done")
        x_ready = sem("x_ready")
        out_done = sem("out_done")
        proj_kept = sem("proj_kept")
        rot_ready = sem("rot_ready")
        rope_done = sem("rope_done")
        score_ready = sem("score_ready")
        nmax_ready = sem("nmax_ready")
        exp_done = sem("exp_done")
        prob_ready = sem("prob_ready")
        probT_ready = sem("probT_ready")
        probT_kept = sem("probT_kept")
        pv_ready = sem("pv_ready")
        yT_hi_ready = sem("yT_hi_ready")
        yT_lo_ready = sem("yT_lo_ready")
        z_ready = sem("z_ready")
        abs_done = sem("abs_done")
        expn_done = sem("expn_done")
        ln1p_done = sem("ln1p_done")
        keepsum_ready = sem("keepsum_ready")
        stick_ready = sem("stick_ready")
        weight_ready = sem("weight_ready")

        def bank_of(i):
            return start_bank if i == 0 else tr_bank

        block = ctx.enter_context(nc.Block())

        def rows_by_tile(w):
            return w.rearrange("(k p) n -> p k n", p=P)

        def ada_view(w):
            return w.rearrange("(p k) n -> p k n", k=8)

        def columns_chunk(w, start):
            return [rows_by_tile(w)[:, half * 4:half * 4 + 4, bass.ds(start, 256)] for half in range(2)]

        def inner_chunk(w, start):
            return [rows_by_tile(w)[:, :, bass.ds(start + half * DFF, P)] for half in range(2)]

        def rows_chunk(w, start):
            return [rows_by_tile(w[bass.ds(start + half * P, P), :]) for half in range(2)]

        def staged(m):
            if m < RAW:
                return raw[:, m, :].rearrange("p (k n) -> p k n", k=2), raw_in[m]
            return ada[:, m % 2, :, :], staged_in[m % 2]

        PROJ = ([(N_QKV + i, w_qkv_a[0], 256 * i) for i in range(12)],
                [(N_KV + i, w_kv_b, 256 * i) for i in range(8)],
                [(N_Q + i, w_q_b[0], 256 * i) for i in range(4)])

        @block.sync
        def _(sp):
            def load(n, halves, at=None):
                if at is not None or n >= RAW:
                    sp.wait_ge(w_lo_ready, n - RAW + 1 if at is None else at + (n - RAW + 1))
                else:
                    sp.wait_ge(acc_steps, 2 * n + 2)
                for half, src in enumerate(halves):
                    dst = raw[:, n % RAW, half * (CH // 2):(half + 1) * (CH // 2)]
                    sp.dma_start(dst.rearrange("p (k n) -> p k n", n=src.shape[2]), src).then_inc(raw_in[n % RAW], 16)

            def load_step(w_in, w_out, n, s, b=None):
                at, c = (None, 0) if b is None else (6 * b, 512 * b)
                load(n + 3 * s - 1, inner_chunk(w_in, c + 256 * s), at)
                load(n + 3 * s, inner_chunk(w_in, c + (256 * s + P)), at)
                load(n + 3 * s + 1, rows_chunk(w_out, c + 256 * (s - 1)), at)

            def load_ffn(f):
                w_in, w_out, n = w_ffn_in[f // 2, f % 2], w_ffn_out[f // 2, f % 2], N_FFN[f]
                load(n, inner_chunk(w_in, 0))
                load(n + 1, inner_chunk(w_in, P))
                peeled = 2 if f == 0 else 0
                for s in range(1, 1 + peeled):
                    load_step(w_in, w_out, n, s)
                if f == 0:
                    sp.dma_start(cst[:, P:], consts[:, P:]).then_inc(cst_in, 16)
                with sp.Fori(0, (STEPS - 1 - peeled) // 2) as b:
                    for s in (1 + peeled, 2 + peeled):
                        load_step(w_in, w_out, n, s, b)
                load(n + FFN_CHUNKS - 1, rows_chunk(w_out, DFF - 256))

            def load_wo(layer):
                for j in range(4):
                    load(N_WO[layer] + j, rows_chunk(w_o[layer], 256 * j))

            sp.dma_start(cond[:, :], c.rearrange("a (p k) -> p (a k)", k=8)).then_inc(c_in, 16)
            for m in range(STAGED):
                dst, landed = staged(m)
                src = ada_view(w_ada[0])[:, 2 * (m % 4):2 * (m % 4) + 2, D * (m // 4):D * (m // 4 + 1)]
                if m < STAGED - 1:
                    sp.dma_start(dst, src).then_inc(landed, 16)
                else:
                    sp.dma_start(dst[:, 0, :], src[:, 0, :]).then_inc(landed, 16)
                    sp.dma_start(dst[:, 1, :], src[:, 1, :]).then_inc(staged_in[2], 16)
                if m == 3:
                    sp.dma_start(cst[:, 0:P], consts[:, 0:P]).then_inc(cst_in, 16)
            for t in range(TT):
                sp.dma_start(x_sb[:, t, :], x[0, t * P:(t + 1) * P, :]).then_inc(x_in, 16)
            load_ffn(0)
            for n, w, at in PROJ[0]:
                load(n, columns_chunk(w, at))
            load_wo(0)
            load_ffn(1)
            for n, w, at in PROJ[1]:
                load(n, columns_chunk(w, at))
            load_ffn(2)
            for n, w, at in PROJ[2]:
                load(n, columns_chunk(w, at))
            load_wo(1)
            load_ffn(3)
            for t in range(TT):
                for half in range(2):
                    sp.wait_ge(x_ready, 2 * 5 + 2 * t + half + 1)
                    cols = slice(half * (D // 2), (half + 1) * (D // 2))
                    sp.dma_start(out[0, t * P:(t + 1) * P, cols], x_sb[:, t, cols]).then_inc(out_done, 16)
            sp.wait_ge(out_done, 64)

        @block.gpsimd
        def _(pool):
            def load_unit(u):
                layer, j = ORDER[u]
                w, b = (w_kv_ada, b_kv_ada) if layer == KV else (w_ada[layer], b_ada[layer])
                if u in GATE_OF:
                    g = GATE_OF.index(u)
                    if g:
                        pool.wait_ge(acc_steps, 8 * GATE_OF[g - 1] + 1)
                    else:
                        pool.wait_ge(set_up, 1)
                    pool.dma_start(bias0[0:1, :], b[j * D:(j + 1) * D].rearrange("(a n) -> a n", a=1))\
                        .then_inc(bias_in, 16)
                for q in range(4):
                    pool.wait_ge(acc_steps, 8 * u + 2 * q - 2)
                    pool.dma_start(ada[:, q % 2, :, :],
                                   ada_view(w)[:, 2 * q:2 * q + 2, j * D:(j + 1) * D])\
                        .then_inc(ada_in[q % 2], 16)

            for u in range(STAGED // 4, UNITS):
                load_unit(u)

        @block.scalar
        def _(act):
            def split_hi(n, at=0, turn=0):
                act.wait_ge(raw_in[n % RAW], 32 * (n // RAW + 1) + 16 + 32 * turn)
                if n >= SPL:
                    act.wait_ge(w_used, n + at - SPL + 1)
                nc.scalar.activation(w_hi[:, n % SPL, :], raw[:, n % RAW, :], ACT.Copy).then_inc(w_hi_ready, 1)

            def silu(f, n, s, t, at=0):
                act.wait_ge(w_used, (n + 3 * s - 1 if s else n) + t + 1 + at)
                nc.scalar.activation(silu_t[:, t, :], gu[t][:, 0:SEQ], ACT.Silu).then_inc(silu_ready, 1)

            def inner_hi(f, s, t, turn=0):
                act.wait_ge(a_ready, 2 * STEPS * f + 2 * s + t + 1 + 4 * turn)
                nc.scalar.activation(a_hi[:, s % 2, t, :], a_full[:, t, :], ACT.Copy).then_inc(a_hi_ready, 1)

            def ffn_step(f, n, s, at=0, turn=0):
                for t in range(2):
                    silu(f, n, s, t, at)
                    split_hi(n + 3 * s + 2 + t, at, turn)
                    inner_hi(f, s, t, turn)
                split_hi(n + 3 * s + 4, at, turn)

            def ffn(f):
                first_unit = FIRST_UNIT[f]
                n = N_FFN[f]
                ffn_step(f, n, 0)
                with act.Fori(0, LOOPS) as b:
                    for s in (1, 2):
                        ffn_step(f, n, s, at=6 * b, turn=b)
                    if first_unit is not None:
                        keep_unit(b + first_unit)
                load_ln_rows(NORM_OF_FFN[f])
                ffn_step(f, n, STEPS - 2)
                s = STEPS - 1
                silu(f, n, s, 0)
                split_hi(n + 3 * s + 2)
                inner_hi(f, s, 0)
                silu(f, n, s, 1)
                if f < 3:
                    split_hi(n + 3 * s + 3)
                inner_hi(f, s, 1)
                nc.scalar.preload_act_table(ACT.Sqrt)
                keep_gate(NORM_OF_FFN[f])

            def keep_unit(u, tiles=KT):
                act.wait_ge(unit_out, u + 1)
                for k in range(tiles):
                    src = misc[k // 4][:, (k % 4) * P:(k % 4 + 1) * P]
                    last = nc.scalar.activation(src, src, ACT.Copy,
                                                accum_out=modT[:, bass.ds(u, 1), k:k + 1].rearrange("p a k -> p (a k)"))
                last.then_inc(mod_ready, 1)

            def load_ln_rows(i):
                if i:
                    act.wait_ge(x_ready, 2 * i)
                act.dma_start(g_row[:, :], ln_g[i // 3, i % 3, :].partition_broadcast(P)).then_inc(ln_row_in, 16)
                act.dma_start(b_row[:, :], ln_b[i // 3, i % 3, :].partition_broadcast(P)).then_inc(ln_row_in, 16)

            def keep_gate(i):
                act.wait_ge(unit_out, GATE_OF[i] + 1)
                nc.scalar.activation(gate[:, :], misc2, ACT.Copy, scale=-GATE_W[i], bias=GATE_W[i])\
                  .then_inc(gate_ready, 1)

            def h_modulate(i, t, hi_too=False):
                act.wait_ge(turned, 4 * i + 2 * t + 1)
                act.wait_ge(coef_ready, i + 1)
                for k in range(KT // 2):
                    last = nc.scalar.activation(h_fulls[t][:, k, :], bank_of(i)[t][0][:, k * P:(k + 1) * P], ACT.Identity,
                                                scale=coef[:, i, 0, k:k + 1], bias=coef[:, i, 1, k:k + 1])
                    if t == 1 and k % 2 == 1:
                        last.then_inc(h_act, 1)
                        if hi_too:
                            h_hi_pair(i, k // 2)
                if t == 0:
                    last.then_inc(h_act, 1)
                elif hi_too:
                    for pair in (2, 3):
                        h_hi_pair(i, pair)

            def h_hi(i, t):
                if t == 1:
                    for pair in range(4):
                        h_hi_pair(i, pair)
                    return
                act.wait_ge(h_act, 3 * i + 1)
                nc.scalar.activation(hT_hi[:, 0:4, 0:P], h_fulls[0][:, 0:4, :], ACT.Copy).then_inc(h_hi_ready, 1)
                act.wait_ge(h_dve, 3 * i + 1)
                nc.scalar.activation(hT_hi[:, 4:8, 0:P], h_fulls[0][:, 4:8, :], ACT.Copy).then_inc(h_hi_ready, 1)

            def h_hi_pair(i, pair):
                act.wait_ge(h_act if pair < 2 else h_dve, 3 * i + 2 + pair % 2)
                k = 2 * pair
                nc.scalar.activation(hT_hi[:, k:k + 2, P:SEQ], h_fulls[1][:, k:k + 2, :], ACT.Copy)\
                  .then_inc(h_hi_ready, 1)

            def deviation(i, t):
                act.wait_ge(mean_ready, 2 * i + t + 1)
                nc.scalar.activation(y_tok[t], z[:, t, :], ACT.Square, bias=nmean[:, t:t + 1],
                                     accum_out=sq[:, t:t + 1]).then_inc(sq_ready, 1)
                act.wait_ge(sq_ready, 2 * i + t + 1)
                nc.scalar.activation(sd[:, t:t + 1], sq[:, t:t + 1], ACT.Sqrt, scale=1.0 / D, bias=eps_t[:, 0:1])\
                  .then_inc(sd_ready, 1)

            def norm(i, h, last_chunk):
                deviation(i, 0)
                h_modulate(h, 0)
                deviation(i, 1)
                h_hi(h, 0)
                h_modulate(h, 1, hi_too=True)
                split_hi(last_chunk + 2)

            def keep_yT(layer, h):
                act.wait_ge(pv_ready, HEADS * layer + h + 1)
                nc.scalar.activation(hT_hi[:, h, :], gu[h % 2][:, 0:SEQ], ACT.Copy).then_inc(yT_hi_ready, 1)

            nc.scalar.preload_act_table(ACT.Silu)
            for r, w in enumerate((ln_g, ln_b)):
                act.dma_start(tmp[0:48, r * P:(r + 1) * P], w.rearrange("l s (k p) -> (l s k) p", p=P))\
                   .then_inc(rows_in, 16)
            for block_, row, b, first, rows in ((0, 0, b_ada[0], 0, 72), (0, 72, b_kv_ada, 0, 8),
                                                (1, 0, b_kv_ada, 8, 8), (1, 8, b_ada[1], 0, 72)):
                act.dma_start(tmp[row:row + rows, (2 + block_) * P:(3 + block_) * P],
                              b.rearrange("(k p) -> k p", p=P)[first:first + rows, :]).then_inc(rows_in, 16)
            act.wait_ge(c_in, 16)
            nc.scalar.activation(cond[:, :], cond[:, :], ACT.Silu).then_inc(cond_ready, 1)
            act.wait_ge(rows_turned, 1)
            nc.scalar.activation(rowsT[:, :], misc[1][:, 0:256], ACT.Copy).then_inc(rows_ready, 1)
            keep_unit(0, KT // 2)
            keep_unit(1, KT // 2)
            h_modulate(0, 0)
            h_hi(0, 0)
            split_hi(0)
            h_modulate(0, 1, hi_too=True)
            split_hi(1)
            ffn(0)
            norm(0, 1, LAST_CHUNK[0])
            n = N_QKV
            for i in range(8):
                split_hi(n + i + 2)
                if i == 3:
                    load_ln_rows(1)
                act.wait_ge(w_used, n + i + 1)
                if i == 0:
                    act.wait_ge(x_ready, 2)
                nc.scalar.activation((qT, kT)[i // 4][:, 2 * (i % 4):2 * (i % 4) + 2, :],
                                     gu[i % 2].rearrange("p (h t) -> p h t", h=2), ACT.Copy).then_inc(proj_kept, 1)
            nc.scalar.preload_act_table(ACT.Exp)

            def keep_v(i):
                act.wait_ge(w_used, n + 8 + i + 1)
                nc.scalar.activation(v_sb[:, :, 256 * i:256 * i + 256],
                                     gu[i % 2].rearrange("p (t n) -> p t n", t=2), ACT.Copy).then_inc(proj_kept, 1)

            def soft_exp(h):
                act.wait_ge(nmax_ready, h + 1)
                if h >= 2:
                    act.wait_ge(probT_ready, h - 1)
                nc.scalar.activation(prob[:, h % 2, 0:P], y[h % 2][:, 0:P], ACT.Exp, scale=SCALE,
                                     bias=nmx[:, h, 0:1], accum_out=rs[:, h, 0:1])
                nc.scalar.activation(prob[:, h % 2, P:384], y[h % 2][:, P:384], ACT.Exp, scale=SCALE,
                                     bias=nmx[:, h, 1:2], accum_out=rs[:, h, 1:2]).then_inc(exp_done, 1)

            def keep_probT(h):
                act.wait_ge(probT_ready, h + 1)
                nc.scalar.activation(qT[:, h, :], y[2 + h % 2][:, 0:SEQ], ACT.Copy)
                nc.scalar.activation(kT[:, h, 0:P], y[2 + h % 2][:, SEQ:384], ACT.Copy).then_inc(probT_kept, 1)

            for i in range(4):
                soft_exp(2 * i)
                soft_exp(2 * i + 1)
                split_hi(n + 8 + i + 2)
                keep_v(i)
                keep_probT(2 * i)
                keep_probT(2 * i + 1)
            for h in range(4):
                keep_yT(0, h)
            keep_gate(1)
            split_hi(N_WO[0] + 2)
            keep_yT(0, 4)
            keep_yT(0, 5)
            split_hi(N_WO[0] + 3)
            keep_yT(0, 6)
            keep_yT(0, 7)
            split_hi(N_WO[0] + 4)
            nc.scalar.preload_act_table(ACT.Sqrt)
            norm(1, 2, LAST_CHUNK[1])
            nc.scalar.preload_act_table(ACT.Silu)
            ffn(1)
            norm(2, 3, LAST_CHUNK[2])
            n = N_KV
            for i in range(8):
                split_hi(n + i + 2)
                if i == 5:
                    h_modulate(4, 0)
                    h_modulate(4, 1)
                if i == 7:
                    act.wait_ge(kv_tile_done, 1)
                    h_hi(4, 0)
                    act.wait_ge(w_used, n + 8)
                    h_hi(4, 1)
                act.wait_ge(w_used, n + i + 1)
                if i < 4:
                    nc.scalar.activation(kT[:, 2 * i:2 * i + 2, :], gu[i % 2].rearrange("p (h t) -> p h t", h=2),
                                         ACT.Copy).then_inc(proj_kept, 1)
                else:
                    nc.scalar.activation(v_sb[:, :, 256 * (i - 4):256 * (i - 4) + 256],
                                         gu[i % 2].rearrange("p (t n) -> p t n", t=2), ACT.Copy)\
                      .then_inc(proj_kept, 1)
            nc.scalar.preload_act_table(ACT.Silu)
            ffn(2)
            norm(3, 5, LAST_CHUNK[3])
            nc.scalar.preload_act_table_set("natural_log_exp_and_others")
            n = N_Q

            def stick_logs(h):
                act.wait_ge(z_ready, h + 1)
                if h >= 4:
                    act.wait_ge(pv_ready, HEADS + h - 3)
                nc.scalar.activation(stick[:, h % 4, :], y[h % 4][:, 0:384], ACT.Abs).then_inc(abs_done, 1)
                act.wait_ge(abs_done, h + 1)
                nc.scalar.activation(stick[:, h % 4, :], stick[:, h % 4, :], ACT.Exp, scale=-1.0).then_inc(expn_done, 1)
                act.wait_ge(expn_done, h + 1)
                nc.scalar.activation(stick[:, h % 4, :], stick[:, h % 4, :], ACT.Ln, bias=1.0).then_inc(ln1p_done, 1)

            def stick_weights(h):
                act.wait_ge(stick_ready, h + 1)
                nc.scalar.activation(stick[:, h % 4, :], y[h % 4][:, 0:384], ACT.Exp).then_inc(weight_ready, 1)

            for i in range(4):
                if i < 3:
                    split_hi(n + i + 2)
                if i == 3:
                    stick_logs(0)
                    stick_logs(1)
                act.wait_ge(w_used, n + i + 1)
                if i == 0:
                    act.wait_ge(x_ready, 2 * 3 + 2)
                nc.scalar.activation(qT[:, 2 * i:2 * i + 2, :], gu[i % 2].rearrange("p (h t) -> p h t", h=2),
                                     ACT.Copy, scale=SCALE).then_inc(proj_kept, 1)
            load_ln_rows(4)
            for h in range(2, HEADS + 3):
                if h < HEADS:
                    stick_logs(h)
                if h <= HEADS + 1:
                    stick_weights(h - 2)
                if h >= 3:
                    keep_yT(1, h - 3)
                if h == HEADS:
                    split_hi(N_WO[1] + 1)
                if h == HEADS + 2:
                    split_hi(N_WO[1] + 2)
            for j in range(1, 3):
                split_hi(N_WO[1] + j + 2)
            nc.scalar.preload_act_table(ACT.Sqrt)
            keep_gate(4)
            norm(4, 6, LAST_CHUNK[4])
            nc.scalar.preload_act_table(ACT.Silu)
            ffn(3)
            deviation(5, 0)
            deviation(5, 1)

        @block.vector
        def _(dve):
            steps = [0]

            def own(instruction):
                steps[0] += 1
                instruction.then_inc(dve_step, 1)
                dve.wait_ge(dve_step, steps[0])

            def split_lo(n, at=0):
                dve.wait_ge(w_hi_ready, n + at + 1)
                nc.vector.tensor_tensor(w_lo[:, n % SPL, :], raw[:, n % RAW, :], w_hi[:, n % SPL, :].bitcast(F32),
                                        ALU.subtract).then_inc(w_lo_ready, 1)

            def accumulate(u, q, gate_i=None):
                sums = acc[:, :]
                if isinstance(u, int) and u < STAGED // 4:
                    src, landed = staged(4 * u + q)
                    dve.wait_ge(landed, 16)
                    if u == 0:
                        sums = acc0
                else:
                    src = ada[:, q % 2, :, :]
                    dve.wait_ge(ada_in[q % 2], 32 * u + (16 * (q // 2) + 16 - 8 * STAGED))
                    if q == 0:
                        dve.wait_ge(unit_out, u)
                for r in range(2):
                    if isinstance(u, int) and 4 * u + q == STAGED - 1 and r == 1:
                        dve.wait_ge(staged_in[2], 16)
                    factor = cond[:, 2 * q + r:2 * q + r + 1]
                    if q == 0 and r == 0:
                        if gate_i is None:
                            nc.vector.tensor_scalar(sums, src[:, r, :], factor, None, ALU.mult).then_inc(acc_steps, 1)
                            continue
                        dve.wait_ge(bias_in, 16 * gate_i + 16)
                        base = bias0[:, :]
                    else:
                        dve.wait_ge(acc_steps, 8 * u + 2 * q + r)
                        base = sums
                    nc.vector.scalar_tensor_tensor(out=sums, in0=src[:, r, :], scalar=factor, in1=base,
                                                   op0=ALU.mult, op1=ALU.add).then_inc(acc_steps, 1)

            def coefficients(i):
                shift, scale, norm_i = H_OF[i]
                dve.wait_ge(mod_ready, kept(scale))
                a, b = coef[:, i, 0, :], coef[:, i, 1, :]
                both = modT[:, shift:scale + 1, :]
                own(nc.vector.tensor_tensor(both, both, biasT[:, BIAS_AT[shift]:BIAS_AT[scale] + 1, :], ALU.add))
                if norm_i is None:
                    nc.vector.tensor_copy(b, modT[:, shift, :])
                    nc.vector.tensor_scalar_add(a, modT[:, scale, :], 1.0).then_inc(coef_ready, 1)
                    return
                g_t = lnT[:, 0, norm_i * KT:(norm_i + 1) * KT]
                b_t = lnT[:, 1, norm_i * KT:(norm_i + 1) * KT]
                own(nc.vector.scalar_tensor_tensor(out=b, in0=modT[:, scale, :], scalar=1.0, in1=b_t,
                                                   op0=ALU.add, op1=ALU.mult))
                own(nc.vector.tensor_tensor(b, b, modT[:, shift, :], ALU.add))
                nc.vector.scalar_tensor_tensor(out=a, in0=modT[:, scale, :], scalar=1.0, in1=g_t,
                                               op0=ALU.add, op1=ALU.mult).then_inc(coef_ready, 1)

            def inner(f, s, t, turn=0):
                dve.wait_ge(silu_ready, 2 * STEPS * f + 2 * s + t + 1 + 4 * turn)
                nc.vector.tensor_tensor(a_full[:, t, :], gu[t][:, SEQ:2 * SEQ], silu_t[:, t, :], ALU.mult)\
                  .then_inc(a_ready, 1)

            def inner_lo(f, s, t, turn=0):
                dve.wait_ge(a_hi_ready, 2 * STEPS * f + 2 * s + t + 1 + 4 * turn)
                nc.vector.tensor_tensor(a_lo[:, s % 2, t, :], a_full[:, t, :], a_hi[:, s % 2, t, :].bitcast(F32),
                                        ALU.subtract).then_inc(a_lo_ready, 1)

            def ffn_step(f, n, s, at=0, turn=0, u=None, parts=((), (), ()), gate_i=None):
                for t in range(2):
                    inner(f, s, t, turn)
                    for q in parts[t]:
                        accumulate(u, q, gate_i)
                    split_lo(n + 3 * s + 2 + t, at)
                    inner_lo(f, s, t, turn)
                for q in parts[2]:
                    accumulate(u, q, gate_i)
                split_lo(n + 3 * s + 4, at)

            def ffn(f, operands):
                n, i, first_unit = N_FFN[f], NORM_OF_FFN[f], FIRST_UNIT[f]
                ffn_step(f, n, 0)
                with dve.Fori(0, LOOPS) as b:
                    if first_unit is None:
                        for s in (1, 2):
                            ffn_step(f, n, s, at=6 * b, turn=b)
                    else:
                        u = b + first_unit
                        ffn_step(f, n, 1, at=6 * b, turn=b, u=u, parts=((0,), (1,), ()))
                        ffn_step(f, n, 2, at=6 * b, turn=b, u=u, parts=((2,), (3,), ()))
                ffn_step(f, n, STEPS - 2, u=GATE_OF[i], parts=((0, 1), (2,), (3,)), gate_i=i)
                s = STEPS - 1
                inner(f, s, 0)
                inner_lo(f, s, 0)
                split_lo(n + 3 * s + 2)
                inner(f, s, 1)
                for h in operands:
                    coefficients(h)
                inner_lo(f, s, 1)
                if f < 3:
                    split_lo(n + 3 * s + 3)

            def h_modulate(i, t, lo_too=False):
                dve.wait_ge(turned, 4 * i + 2 * t + 2)
                dve.wait_ge(coef_ready, i + 1)
                for k in range(KT // 2, KT):
                    last = nc.vector.tensor_scalar(h_fulls[t][:, k, :], bank_of(i)[t][1][:, (k - 4) * P:(k - 3) * P],
                                                   coef[:, i, 0, k:k + 1], coef[:, i, 1, k:k + 1], ALU.mult, ALU.add)
                    if t == 1 and k % 2 == 1:
                        last.then_inc(h_dve, 1)
                        if lo_too:
                            h_lo_pair(i, k // 2 - 2)
                if t == 0:
                    last.then_inc(h_dve, 1)
                elif lo_too:
                    h_lo_half(i, 1)
                    for pair in (2, 3):
                        h_lo_pair(i, pair)

            def h_lo_half(i, half):
                dve.wait_ge(h_hi_ready, 6 * i + half + 1)
                nc.vector.tensor_tensor(hT_lo[:, 4 * half:4 * half + 4, 0:P],
                                        h_fulls[0][:, 4 * half:4 * half + 4, :],
                                        hT_hi[:, 4 * half:4 * half + 4, 0:P].bitcast(F32),
                                        ALU.subtract).then_inc(h_lo_ready, 1)

            def h_lo_pair(i, pair):
                dve.wait_ge(h_hi_ready, 6 * i + 2 + pair + 1)
                k = 2 * pair
                nc.vector.tensor_tensor(hT_lo[:, k:k + 2, P:SEQ], h_fulls[1][:, k:k + 2, :],
                                        hT_hi[:, k:k + 2, P:SEQ].bitcast(F32), ALU.subtract).then_inc(h_lo_ready, 1)

            def residual(t, c0, width, part):
                cols = slice(c0, c0 + width)
                own(nc.vector.tensor_tensor(z[:, t, cols], y_tok[t][:, cols], gate[:, cols], ALU.mult))
                own(nc.vector.scalar_tensor_tensor(out=z[:, t, cols], in0=x_sb[:, t, cols], scalar=ALPHA,
                                                   in1=z[:, t, cols], op0=ALU.mult, op1=ALU.add,
                                                   accum_out=total[:, part:part + 1]))

            def residual_first(i):
                dve.wait_ge(gate_ready, i + 1)
                dve.wait_ge(y_ready, 2 * i + 1)
                residual(0, 0, D, 0)
                nc.vector.tensor_scalar(nmean[:, 0:1], total[:, 0:1], -1.0 / D, None, ALU.mult).then_inc(mean_ready, 1)
                dve.wait_ge(y_ready, 2 * i + 2)
                residual(1, 0, D // 2, 1)

            def residual_second(i):
                dve.wait_ge(w_used, LAST_CHUNK[i] + 1)
                residual(1, D // 2, D // 2, 2)
                nc.vector.tensor_scalar(nmean[:, 1:2], total[:, 1:2], total[:, 2:3], -1.0 / D, ALU.add, ALU.mult)\
                  .then_inc(mean_ready, 1)

            def normalise(i, t):
                dve.wait_ge(sd_ready, 2 * i + t + 1)
                own(nc.vector.reciprocal(rstd[:, t:t + 1], sd[:, t:t + 1]))
                for half in range(2):
                    part = z[:, t, half * (D // 2):(half + 1) * (D // 2)]
                    nc.vector.tensor_scalar(part, part, nmean[:, t:t + 1], rstd[:, t:t + 1],
                                            ALU.add, ALU.mult).then_inc(xn_ready, 1)

            def x_scaled(i, t):
                dve.wait_ge(ln_row_in, 32 * (i + 1))
                dve.wait_ge(xn_ready, 4 * i + 2 * t + 2)
                nc.vector.tensor_tensor(x_sb[:, t, :], z[:, t, :], g_row[:, :], ALU.mult).then_inc(x_scaled_done, 1)

            def x_shifted(i, t):
                dve.wait_ge(x_scaled_done, 2 * i + t + 1)
                nc.vector.tensor_tensor(x_sb[:, t, :], x_sb[:, t, :], b_row[:, :], ALU.add).then_inc(x_ready, 1)

            def norm(i, h, last_chunk):
                residual_first(i)
                normalise(i, 0)
                residual_second(i)
                h_modulate(h, 0)
                normalise(i, 1)
                h_lo_half(h, 0)
                h_modulate(h, 1, lo_too=True)
                x_scaled(i, 0)
                split_lo(last_chunk + 2)
                x_shifted(i, 0)
                x_scaled(i, 1)
                x_shifted(i, 1)

            def last_norm(i):
                def centred(t):
                    nc.vector.scalar_tensor_tensor(out=x_sb[:, t, :], in0=z[:, t, :], scalar=nmean[:, t:t + 1],
                                                   in1=g_row[:, :], op0=ALU.add, op1=ALU.mult).then_inc(centre_done, 1)

                def scaled(t):
                    dve.wait_ge(sd_ready, 2 * i + t + 1)
                    own(nc.vector.reciprocal(rstd[:, t:t + 1], sd[:, t:t + 1]))
                    dve.wait_ge(centre_done, t + 1)
                    for half in range(2):
                        cols = slice(half * (D // 2), (half + 1) * (D // 2))
                        nc.vector.scalar_tensor_tensor(out=x_sb[:, t, cols], in0=x_sb[:, t, cols],
                                                       scalar=rstd[:, t:t + 1], in1=b_row[:, cols],
                                                       op0=ALU.mult, op1=ALU.add).then_inc(x_ready, 1)

                residual_first(i)
                dve.wait_ge(ln_row_in, 32 * (i + 1))
                dve.wait_ge(mean_ready, 2 * i + 1)
                centred(0)
                residual_second(i)
                dve.wait_ge(mean_ready, 2 * i + 2)
                centred(1)
                scaled(0)
                scaled(1)

            def keep_yT(layer, h):
                dve.wait_ge(yT_hi_ready, HEADS * layer + h + 1)
                nc.vector.tensor_tensor(hT_lo[:, h, :], gu[h % 2][:, 0:SEQ], hT_hi[:, h, :].bitcast(F32),
                                        ALU.subtract).then_inc(yT_lo_ready, 1)

            def keep_second_half(u):
                dve.wait_ge(unit_out, u + 1)
                nc.vector.reduce_sum(modT[:, u, KT // 2:KT], misc[1].rearrange("p (k n) -> p k n", n=P), AX.X)\
                  .then_inc(second_half_kept, 1)

            nc.vector.memset(eps_t[:, :], EPS)
            nc.vector.memset(neg_ones[:, :], -1.0)
            nc.vector.memset(zeros[:, :], 0.0)
            nc.vector.memset(bias0[:, :], 0.0).then_inc(set_up, 1)
            dve.wait_ge(cond_ready, 1)
            for u in range(2):
                for q in range(4):
                    accumulate(u, q)
                    if u == 1 and q == 0:
                        keep_second_half(0)
            keep_second_half(1)
            dve.wait_ge(rows_ready, 1)
            dve.wait_ge(second_half_kept, 2)
            coefficients(0)
            h_modulate(0, 0)
            h_modulate(0, 1)
            h_lo_half(0, 0)
            split_lo(0)
            for pair in range(4):
                if pair == 2:
                    h_lo_half(0, 1)
                h_lo_pair(0, pair)
            split_lo(1)
            ffn(0, (1,))
            norm(0, 1, LAST_CHUNK[0])
            n = N_QKV

            def rope(i):
                side = (qT, kT)[i // 4][0:ROT, 2 * (i % 4):2 * (i % 4) + 2, :]
                two = [ROT, 2, SEQ]
                dve.wait_ge(rot_ready, i + 1)
                if i:
                    dve.wait_ge(rope_done, i)
                own(nc.vector.tensor_tensor(rope_t.rearrange("p (h t) -> p h t", h=2),
                                            misc[i % 2][0:ROT, :].rearrange("p (h t) -> p h t", h=2),
                                            sin_t.unsqueeze(1).to_broadcast(two), ALU.mult))
                own(nc.vector.tensor_tensor(side, side, cos_t.unsqueeze(1).to_broadcast(two), ALU.mult))
                nc.vector.tensor_tensor(side, side, rope_t.rearrange("p (h t) -> p h t", h=2), ALU.add)\
                  .then_inc(rope_done, 1)

            for i in range(8):
                split_lo(n + i + 2)
                if i >= 1:
                    rope(i - 1)
                if i == 0:
                    dve.wait_ge(cst_in, 32)
                    for m, mask in enumerate((ident, causal, strict)):
                        last = nc.vector.tensor_copy(masks[:, m, :], mask)
                    last.then_inc(masks_ready, 1)
                if 2 <= i < 6:
                    accumulate(GATE_OF[1], i - 2, 1)

            def soft_max(h):
                dve.wait_ge(score_ready, h + 1)
                nc.vector.reduce_max(mx[:, h, 0:1], y[h % 2][:, 0:P], AX.X)
                own(nc.vector.reduce_max(mx[:, h, 1:2], y[h % 2][:, P:384], AX.X))
                nc.vector.tensor_scalar(nmx[:, h, :], mx[:, h, :], -SCALE, None, ALU.mult).then_inc(nmax_ready, 1)

            def soft_scale(h):
                dve.wait_ge(exp_done, h + 1)
                own(nc.vector.reciprocal(rinv[:, h, :], rs[:, h, :]))
                nc.vector.tensor_scalar(prob[:, h % 2, 0:P], prob[:, h % 2, 0:P], rinv[:, h, 0:1], None, ALU.mult)
                nc.vector.tensor_scalar(prob[:, h % 2, P:384], prob[:, h % 2, P:384], rinv[:, h, 1:2], None,
                                        ALU.mult).then_inc(prob_ready, 1)

            for i in range(4):
                soft_max(2 * i)
                soft_max(2 * i + 1)
                if i == 0:
                    rope(7)
                soft_scale(2 * i)
                soft_scale(2 * i + 1)
                split_lo(n + 8 + i + 2)
            coefficients(2)
            for h in range(4):
                keep_yT(0, h)
            split_lo(N_WO[0] + 2)
            keep_yT(0, 4)
            keep_yT(0, 5)
            split_lo(N_WO[0] + 3)
            keep_yT(0, 6)
            keep_yT(0, 7)
            split_lo(N_WO[0] + 4)
            norm(1, 2, LAST_CHUNK[1])
            ffn(1, (3,))
            norm(2, 3, LAST_CHUNK[2])
            for i in range(8):
                split_lo(N_KV + i + 2)
                if i == 2:
                    coefficients(4)
                if i == 5:
                    for t in range(TT):
                        h_modulate(4, t)
            h_lo_half(4, 0)
            for pair in range(4):
                if pair == 2:
                    h_lo_half(4, 1)
                h_lo_pair(4, pair)
            ffn(2, (5,))
            norm(3, 5, LAST_CHUNK[3])
            for i in range(3):
                split_lo(N_Q + i + 2)
                if i > 0:
                    accumulate(GATE_OF[4], i - 1, 4)

            def stick_sums(h):
                dve.wait_ge(ln1p_done, h + 1)
                if h >= 2:
                    dve.wait_ge(stick_ready, h - 1)
                own(nc.vector.scalar_tensor_tensor(out=sp_t[:, h % 2, :], in0=y[h % 4][:, 0:384], scalar=0.0,
                                                   in1=stick[:, h % 4, :], op0=ALU.max, op1=ALU.add))
                nc.vector.tensor_tensor(sp_t[:, h % 2, 0:P], sp_t[:, h % 2, 0:P], keep, ALU.mult)
                nc.vector.tensor_tensor(sp_t[:, h % 2, SEQ:384], sp_t[:, h % 2, SEQ:384], keep, ALU.mult)\
                  .then_inc(keepsum_ready, 1)

            for h in range(HEADS + 3):
                if h < HEADS:
                    stick_sums(h)
                if h == 1 or h == 3:
                    accumulate(GATE_OF[4], 2 + h // 2, 4)
                if h >= 3:
                    keep_yT(1, h - 3)
                if h == HEADS:
                    split_lo(N_WO[1] + 1)
                if h == HEADS + 2:
                    split_lo(N_WO[1] + 2)
                if h == 6:
                    coefficients(6)
            for j in range(1, 3):
                split_lo(N_WO[1] + j + 2)
            norm(4, 6, LAST_CHUNK[4])
            ffn(3, ())
            last_norm(5)

        @block.tensor
        def _(pe):
            def three(dst, stat, mov, start, stop):
                (s_hi, s_lo), (m_hi, m_lo) = stat, mov
                nc.tensor.matmul(dst, s_hi, m_hi, start=start, stop=False)
                nc.tensor.matmul(dst, s_hi, m_lo, start=False, stop=False)
                return nc.tensor.matmul(dst, s_lo, m_hi, start=False, stop=stop)

            def w_cols(n, k, j, inner):
                at, width = (j * 1024 + k * P if inner else k * 256 + j * P), P
                return w_hi[:, n % SPL, at:at + width], w_lo[:, n % SPL, at:at + width]

            def w_wide(n, k):
                at = k * 256
                return w_hi[:, n % SPL, at:at + 256], w_lo[:, n % SPL, at:at + 256]

            def w_rows(n, j, half):
                at = j * 1024 + half * 512
                return w_hi[:, n % SPL, at:at + 512], w_lo[:, n % SPL, at:at + 512]

            def h_all(k):
                return hT_hi[:, k, :], hT_lo[:, k, :]

            def h_tok(k, t):
                return hT_hi[:, k, t * P:(t + 1) * P], hT_lo[:, k, t * P:(t + 1) * P]

            def turn_tile(src, t, ready=None, banks=tr_bank):
                for k in range(KT):
                    if ready and k % 4 == 0:
                        pe.wait_ge(ready[0], ready[1] + k // 4)
                    last = nc.tensor.transpose(banks[t][k // 4][:, (k % 4) * P:(k % 4 + 1) * P],
                                               src[:, t, k * P:(k + 1) * P], ident)
                    if k % 4 == 3:
                        last.then_inc(turned, 1)

            def turn_unit(u, sums=acc):
                pe.wait_ge(acc_steps, 8 * u + 8)
                for k in range(KT):
                    last = nc.tensor.transpose(misc[k // 4][:, (k % 4) * P:(k % 4 + 1) * P],
                                               sums[:, k * P:(k + 1) * P], ident)
                last.then_inc(unit_out, 1)

            def spread_gate(i):
                pe.wait_ge(acc_steps, 8 * GATE_OF[i] + 8)
                for half in range(2):
                    last = nc.tensor.matmul(misc[half], neg_ones[:, :], acc[:, half * 512:(half + 1) * 512],
                                            start=True, stop=True)
                last.then_inc(unit_out, 1)

            def columns_out(n, dst, inner=False, at=0, h=None):
                pe.wait_ge(w_lo_ready, n + at + 1)
                for j in range(2):
                    for k in range(KT):
                        if h is not None and j == 0 and k % 2 == 0:
                            pe.wait_ge(h_lo_ready, 6 * h + (2, 3, 5, 6)[k // 2])
                        last = three(dst[:, j * SEQ:(j + 1) * SEQ], w_cols(n, k, j, inner), h_all(k),
                                     k == 0, k == KT - 1)
                last.then_inc(w_used, 1)

            def tokens_out(n, dst, signal_first=False):
                pe.wait_ge(w_lo_ready, n + 1)
                for t in range(TT):
                    for k in range(KT):
                        last = three(dst[:, t * 256:(t + 1) * 256], h_tok(k, t), w_wide(n, k),
                                     k == 0, k == KT - 1)
                    if t == 0 and signal_first:
                        last.then_inc(kv_tile_done, 1)
                last.then_inc(w_used, 1)

            def clear(bank):
                nc.tensor.matmul(bank, zeros[:, 0:P], zeros[:, :], start=True, stop=False)

            def stay_busy(times):
                for _ in range(times):
                    nc.tensor.matmul(gu[0], zeros[:, 0:P], zeros[:, :], start=True, stop=True)

            def first_pair(n, h, src, ready, inner=False):
                if src is not None:
                    for t in range(TT):
                        turn_tile(src, t, ready(t))
                        if inner and t == 1:
                            clear(y[2])
                            clear(y[3])
                        stay_busy(WAIT_PRODUCTS[t] - (2 if inner and t == 1 else 0))
                for c in range(2):
                    if c == 1 and n == N_FFN[2]:
                        pe.wait_ge(proj_kept, 20)
                    columns_out(n + c, gu[c], inner, h=None if c else h)

            def add_rows(n, operand, t, first=False, last=False, halves=(0, 1)):
                for j in range(2):
                    hi, lo = operand(j, t)
                    for half in halves:
                        m = w_rows(n, j, half)
                        dst = y[2 * t + half]
                        nc.tensor.matmul(dst, hi, m[0], start=first and j == 0, stop=False)
                        nc.tensor.matmul(dst, hi, m[1], start=False, stop=False)
                        end = nc.tensor.matmul(dst, lo, m[0], start=False, stop=last and j == 1)
                return end

            def last_pair(n, operands, waits):
                for c in range(2):
                    pe.wait_ge(w_lo_ready, n + c + 1)
                    pe.wait_ge(*waits[c])
                    end = add_rows(n + c, operands[c], 0, last=c == 1)
                end.then_inc(y_ready, 1)
                for half in range(2):
                    for c in range(2):
                        end = add_rows(n + c, operands[c], 1, last=c == 1, halves=(half,))
                        if half == 1:
                            end.then_inc(w_used, 1)
                    if half == 0:
                        end.then_inc(y_ready, 1)

            def in_tile(f, n, s, t, at=0, turn=0):
                pe.wait_ge(a_ready, 2 * STEPS * f + 2 * s + t - 1 + 4 * turn)
                columns_out(n + 3 * s - 1 + t, gu[t], inner=True, at=at)

            def inner(s):
                return lambda j, t: (a_hi[:, s % 2, j, t * P:(t + 1) * P], a_lo[:, s % 2, j, t * P:(t + 1) * P])

            def inner_done(f, s, turn=0):
                return a_lo_ready, 2 * STEPS * f + 2 * s + 2 + 4 * turn

            def ffn_out(f, n, s, at=0, turn=0):
                pe.wait_ge(*inner_done(f, s, turn))
                pe.wait_ge(w_lo_ready, n + 3 * s + 4 + at + 1)
                add_rows(n + 3 * s + 4, inner(s), 0)
                add_rows(n + 3 * s + 4, inner(s), 1).then_inc(w_used, 1)

            def ffn(f, src, ready):
                n, first_unit = N_FFN[f], FIRST_UNIT[f]
                first_pair(n, H_OF_FFN[f], src, ready, inner=True)
                for i in range(4 if src is None else 2):
                    clear(y[i])
                with pe.Fori(0, LOOPS) as b:
                    for s in (1, 2):
                        for t in range(2):
                            in_tile(f, n, s, t, at=6 * b, turn=b)
                        ffn_out(f, n, s - 1, at=6 * b, turn=b)
                    if first_unit is not None:
                        turn_unit(b + first_unit)
                for t in range(2):
                    in_tile(f, n, STEPS - 2, t)
                ffn_out(f, n, STEPS - 3)
                for t in range(2):
                    in_tile(f, n, STEPS - 1, t)
                pe.wait_ge(mod_ready, kept(GATE_OF[NORM_OF_FFN[f]]))
                spread_gate(NORM_OF_FFN[f])
                last_pair(n + FFN_CHUNKS - 2, (inner(STEPS - 2), inner(STEPS - 1)),
                          (inner_done(f, STEPS - 2), inner_done(f, STEPS - 1)))

            def normed(i):
                return lambda t: (xn_ready, 4 * i + 2 * t + 1)

            def weigh_values(layer, h, first, second):
                if layer == 0:
                    pe.wait_ge(probT_kept, h + 1)
                if h >= 2:
                    pe.wait_ge(yT_lo_ready, HEADS * layer + h - 1)
                nc.tensor.matmul(gu[h % 2][:, 0:SEQ], v_sb[:, 0, h * DH:(h + 1) * DH], first, start=True, stop=False)
                nc.tensor.matmul(gu[h % 2][:, P:SEQ], v_sb[:, 1, h * DH:(h + 1) * DH], second, start=False, stop=True)\
                  .then_inc(pv_ready, 1)

            def heads_pair(j):
                return lambda jj, t: h_tok(2 * j + jj, t)

            def output_rows(layer, j):
                pe.wait_ge(yT_lo_ready, HEADS * layer + 2 * j + 2)
                pe.wait_ge(w_lo_ready, N_WO[layer] + j + 1)
                add_rows(N_WO[layer] + j, heads_pair(j), 0, first=j == 0)
                add_rows(N_WO[layer] + j, heads_pair(j), 1, first=j == 0).then_inc(w_used, 1)

            def output_end(layer):
                last_pair(N_WO[layer] + 2, (heads_pair(2), heads_pair(3)),
                          ((yT_lo_ready, HEADS * layer + 6), (yT_lo_ready, HEADS * layer + 8)))

            pe.wait_ge(set_up, 1)
            pe.wait_ge(cst_in, 16)
            pe.wait_ge(rows_in, 96)
            for r in range(2):
                last = nc.tensor.transpose(misc[1][:, 48 * r:48 * r + 48], tmp[0:48, r * P:(r + 1) * P],
                                           ident[0:48, 0:48])
            for block_ in range(2):
                last = nc.tensor.transpose(misc[1][:, 96 + 80 * block_:176 + 80 * block_],
                                           tmp[0:80, (2 + block_) * P:(3 + block_) * P], ident[0:80, 0:80])
            last.then_inc(rows_turned, 1)
            pe.wait_ge(rows_ready, 1)
            turn_unit(0, acc0)
            stay_busy(START_PRODUCTS[0])
            pe.wait_ge(mod_ready, 1)
            pe.wait_ge(second_half_kept, 1)
            turn_unit(1)
            pe.wait_ge(x_in, 16 * TT)
            turn_tile(x_sb, 0, banks=start_bank)
            turn_tile(x_sb, 1, banks=start_bank)
            stay_busy(START_PRODUCTS[1])
            ffn(0, None, None)

            def rotate(i):
                pe.wait_ge(proj_kept, i + 1)
                if i >= 2:
                    pe.wait_ge(rope_done, i - 1)
                nc.tensor.matmul(misc[i % 2], rot_m,
                                 (qT, kT)[i // 4][0:ROT, 2 * (i % 4):2 * (i % 4) + 2, :].rearrange("p h t -> p (h t)"),
                                 start=True, stop=True).then_inc(rot_ready, 1)

            first_pair(N_QKV, 1, z, normed(0))
            pe.wait_ge(cst_in, 32)
            rotate(0)
            for i in range(2, 8):
                pe.wait_ge(proj_kept, i - 1)
                columns_out(N_QKV + i, gu[i % 2])
                rotate(i - 1)

            def scores(h):
                pe.wait_ge(rope_done, 4 + h // 2 + 1)
                if h >= 2:
                    pe.wait_ge(exp_done, h - 1)
                s = y[h % 2]
                nc.tensor.matmul(s[:, 0:P], qT[:, h, 0:P], kT[:, h, 0:P], start=True, stop=False)
                nc.tensor.matmul(s[:, 0:P], ident_b, causal_b, start=False, stop=True)
                nc.tensor.matmul(s[:, P:384], qT[:, h, P:SEQ], kT[:, h, :], start=True, stop=False)
                nc.tensor.matmul(s[:, SEQ:384], ident_b, causal_b, start=False, stop=True).then_inc(score_ready, 1)

            def turn_probs(h):
                pe.wait_ge(prob_ready, h + 1)
                if h >= 2:
                    pe.wait_ge(probT_kept, h - 1)
                for b in range(3):
                    last = nc.tensor.transpose(y[2 + h % 2][:, b * P:(b + 1) * P], prob[:, h % 2, b * P:(b + 1) * P],
                                               ident)
                last.then_inc(probT_ready, 1)

            def values_out(i):
                pe.wait_ge(proj_kept, 8 + i - 1)
                tokens_out(N_QKV + 8 + i, gu[i % 2])

            pe.wait_ge(masks_ready, 1)
            for i in range(4):
                scores(2 * i)
                scores(2 * i + 1)
                if i == 0:
                    rotate(7)
                values_out(i)
                turn_probs(2 * i)
                turn_probs(2 * i + 1)
            pe.wait_ge(proj_kept, 12)
            for h in range(4):
                weigh_values(0, h, qT[:, h, :], kT[:, h, 0:P])
            spread_gate(1)
            for j in range(2):
                output_rows(0, j)
                for h in (2 * j + 4, 2 * j + 5):
                    weigh_values(0, h, qT[:, h, :], kT[:, h, 0:P])
            output_end(0)
            ffn(1, z, normed(1))
            first_pair(N_KV, 3, z, normed(2))
            for i in range(2, 8):
                if i == 4:
                    pe.wait_ge(x_ready, 2 * 2 + 2)
                    turn_tile(x_sb, 0)
                    turn_tile(x_sb, 1)
                pe.wait_ge(proj_kept, 12 + i - 1)
                if i < 4:
                    columns_out(N_KV + i, gu[i % 2])
                else:
                    tokens_out(N_KV + i, gu[i % 2], signal_first=i == 7)
            pe.wait_ge(proj_kept, 19)
            ffn(2, None, None)
            first_pair(N_Q, 5, z, normed(3))

            def stick_scores(h):
                s = y[h % 4]
                nc.tensor.matmul(s[:, 0:SEQ], kT[:, h, 0:P], qT[:, h, :], start=True, stop=True)
                nc.tensor.matmul(s[:, SEQ:384], kT[:, h, P:SEQ], qT[:, h, P:SEQ], start=False, stop=True,
                                 skip_group_check=True).then_inc(z_ready, 1)

            def stick_log_weights(h):
                pe.wait_ge(keepsum_ready, h + 1)
                s, first, second = y[h % 4], sp_t[:, h % 2, 0:SEQ], sp_t[:, h % 2, SEQ:384]
                for dst, stat, mov in ((s[:, 0:SEQ], tri, first), (s[:, P:SEQ], neg_ones[:, :], second),
                                       (s[:, SEQ:384], tri, second), (s[:, 0:P], ident_b, strict_b),
                                       (s[:, SEQ:384], ident_b, strict_b)):
                    last = nc.tensor.matmul(dst, stat, mov, start=False, stop=True, skip_group_check=True)
                last.then_inc(stick_ready, 1)

            for h in range(HEADS + 3):
                if h == 0:
                    pe.wait_ge(proj_kept, 21)
                    columns_out(N_Q + 2, gu[0])
                if h == 2:
                    pe.wait_ge(proj_kept, 22)
                    columns_out(N_Q + 3, gu[1])
                if h < HEADS:
                    pe.wait_ge(proj_kept, 21 + h // 2)
                    stick_scores(h)
                if 2 <= h <= HEADS + 1:
                    stick_log_weights(h - 2)
                if h == HEADS:
                    spread_gate(4)
                if h >= 3:
                    pe.wait_ge(weight_ready, h - 2)
                    weigh_values(1, h - 3, stick[:, (h - 3) % 4, 0:SEQ], stick[:, (h - 3) % 4, SEQ:384])
            for j in range(2):
                output_rows(1, j)
            output_end(1)
            ffn(3, z, normed(4))


_INS = ["x", "c", "w_ada", "b_ada", "ln_g", "ln_b", "w_ffn_in", "w_ffn_out", "w_qkv_a", "w_q_b",
        "w_kv_ada", "b_kv_ada", "w_kv_b", "w_o"]


def shape_constants():
    row, col = np.arange(P)[:, None], np.arange(P)[None, :]
    a = np.zeros((P, C_ALL), np.float32)
    a[:, C_ID:C_ID + P] = row == col
    a[:, C_TRI:C_TRI + P] = np.where(row >= col, -1.0, 0.0)
    a[:, C_CAUSAL:C_CAUSAL + P] = np.where(col > row, -1e30, 0.0)
    a[:, C_STRICT:C_STRICT + P] = np.where(row >= col, -1e30, 0.0)
    a[:, C_KEEP:C_KEEP + P] = row < col
    half = ROT // 2
    freq = np.power(np.float32(500000.0), -np.arange(half, dtype=np.float32) * np.float32(2.0) / np.float32(ROT))
    angle = np.arange(SEQ, dtype=np.float32)[None, :] * freq.astype(np.float32)[:, None]
    for i in range(2):
        a[i * half:(i + 1) * half, C_COS:C_COS + SEQ] = np.cos(angle)
        a[i * half:(i + 1) * half, C_SIN:C_SIN + SEQ] = np.sin(angle)
    for i in range(half):
        a[i + half, C_ROT + i] = -1.0
        a[i, C_ROT + i + half] = 1.0
    return a


def kernel(**inputs):
    import concourse.bacc as bacc
    from concourse.bass_utils import run_bass_kernel_spmd

    nc = bacc.Bacc("TRN2", target_bir_lowering=False, num_devices=1)
    arrays, args = {}, []
    for name in _INS:
        a = np.ascontiguousarray(inputs[name])
        arrays["in_" + name] = a
        args.append(nc.dram_tensor("in_" + name, a.shape, mybir.dt.from_np(a.dtype), kind="ExternalInput").ap())
    arrays["in_consts"] = shape_constants()
    args.append(nc.dram_tensor("in_consts", (P, C_ALL), F32, kind="ExternalInput").ap())
    args.append(nc.dram_tensor("out", (1, SEQ, D), F32, kind="ExternalOutput").ap())
    build(nc, *args)
    r = run_bass_kernel_spmd(nc, [arrays], core_ids=[0])
    return r.results[0]["out"]
```
